# Optimizing a Trainium2 kernel written in Bass

```python
import math
import jax, jax.numpy as jnp
from jax import lax
import numpy as np

D_MODEL = 1024
BATCH = 1
SEQ = 1024
DEPTH = 1

N_MIXERS = 2
N_ATTN_LAYERS = (DEPTH + N_MIXERS - 1) // N_MIXERS
N_CONV_LAYERS = DEPTH // N_MIXERS
HEAD_DIM = 64
N_Q_HEADS = D_MODEL // HEAD_DIM
N_KV_HEADS = 4
GQA_GROUP = N_Q_HEADS // N_KV_HEADS
WINDOW = 128
Q_DIM = N_Q_HEADS * HEAD_DIM
KV_DIM = N_KV_HEADS * HEAD_DIM
QKV_DIM = Q_DIM + 2 * KV_DIM
NUM_BUCKETS = 32
MAX_EXACT = NUM_BUCKETS // 2
MAX_DISTANCE = 128
CONV_CHANNELS = D_MODEL
CONV_WIDTH = 31
N_EXPERTS = 32
TOP_K = 4
D_EXPERT = D_MODEL
SWIGLU_LIMIT = 7.0
SWIGLU_ALPHA = 1.702
EXPERT_BLOCK = 128
NORM_EPS = 1e-5
NEG_INF = -1e30

kernel_name = "hybrid_swa_conformer_moe_adaln"

def _rmsnorm(x, g):
    xf = x.astype(jnp.float32)
    y = xf * lax.rsqrt(jnp.mean(xf * xf, axis=-1, keepdims=True) + NORM_EPS)
    return (y * g.astype(jnp.float32)).astype(x.dtype)

def _layernorm(x, g, b):
    xf = x.astype(jnp.float32)
    mu = jnp.mean(xf, axis=-1, keepdims=True)
    var = jnp.mean(jnp.square(xf - mu), axis=-1, keepdims=True)
    y = (xf - mu) * lax.rsqrt(var + NORM_EPS)
    return (y * g.astype(jnp.float32) + b.astype(jnp.float32)).astype(x.dtype)

def _band_geometry():
    dist = jnp.arange(WINDOW)[:, None] + WINDOW - jnp.arange(2 * WINDOW)[None, :]
    n = jnp.maximum(dist, 0)
    nf = jnp.maximum(n, 1).astype(jnp.float32)
    large = MAX_EXACT + (jnp.log(nf / MAX_EXACT) / math.log(MAX_DISTANCE / MAX_EXACT)
                         * (NUM_BUCKETS - MAX_EXACT)).astype(jnp.int32)
    large = jnp.minimum(large, NUM_BUCKETS - 1)
    bucket = jnp.where(n < MAX_EXACT, n, large)
    return dist, bucket

def _rel_bias(table):
    _, bucket = _band_geometry()
    bias = table[bucket]
    return jnp.transpose(bias, (2, 0, 1)).reshape(N_KV_HEADS, GQA_GROUP, WINDOW, 2 * WINDOW)

def _sliding_window_attention(h, w_qkv, b_qkv, w_o, b_o, sinks, rel_bias):
    bsz, seq, _ = h.shape
    nb = seq // WINDOW
    qkv = h @ w_qkv + b_qkv
    q, k, v = jnp.split(qkv, [Q_DIM, Q_DIM + KV_DIM], axis=-1)
    q = q.reshape(bsz, nb, WINDOW, N_KV_HEADS, GQA_GROUP, HEAD_DIM) * (HEAD_DIM ** -0.5)
    k = k.reshape(bsz, nb, WINDOW, N_KV_HEADS, HEAD_DIM)
    v = v.reshape(bsz, nb, WINDOW, N_KV_HEADS, HEAD_DIM)
    pad = ((0, 0), (1, 0), (0, 0), (0, 0), (0, 0))
    kw = jnp.concatenate([jnp.pad(k, pad)[:, :-1], k], axis=2)
    vw = jnp.concatenate([jnp.pad(v, pad)[:, :-1], v], axis=2)
    scores = jnp.einsum('bnqhgd,bnshd->bnhgqs', q, kw).astype(jnp.float32)
    scores = scores + rel_bias.astype(jnp.float32)[None, None]
    dist, _ = _band_geometry()
    in_window = (dist >= 0) & (dist < WINDOW)
    key_pos = jnp.arange(nb)[:, None] * WINDOW + jnp.arange(2 * WINDOW)[None, :] - WINDOW
    valid = in_window[None] & (key_pos >= 0)[:, None, :]
    scores = jnp.where(valid[None, :, None, None], scores, NEG_INF)
    sink = sinks.astype(jnp.float32).reshape(N_KV_HEADS, GQA_GROUP)[None, None, :, :, None, None]
    sink = jnp.broadcast_to(sink, scores.shape[:-1] + (1,))
    probs = jax.nn.softmax(jnp.concatenate([scores, sink], axis=-1), axis=-1)[..., :-1]
    out = jnp.einsum('bnhgqs,bnshd->bnqhgd', probs.astype(vw.dtype), vw)
    return out.reshape(bsz, seq, Q_DIM) @ w_o + b_o

def _conformer_conv(h, w_in, b_in, w_dw, b_dw, ln_g, ln_b, w_out, b_out):
    u = h @ w_in + b_in
    a, g = jnp.split(u, 2, axis=-1)
    u = a * jax.nn.sigmoid(g)
    y = lax.conv_general_dilated(u, w_dw[:, None, :], window_strides=(1,),
                                 padding=[(CONV_WIDTH - 1, 0)],
                                 dimension_numbers=('NWC', 'WIO', 'NWC'),
                                 feature_group_count=CONV_CHANNELS) + b_dw
    y = jax.nn.silu(_layernorm(y, ln_g, ln_b))
    return y @ w_out + b_out

def _clamped_swiglu(u):
    glu, lin = jnp.split(u, 2, axis=-1)
    glu = jnp.minimum(glu, SWIGLU_LIMIT)
    lin = jnp.clip(lin, -SWIGLU_LIMIT, SWIGLU_LIMIT)
    return glu * jax.nn.sigmoid(SWIGLU_ALPHA * glu) * (lin + 1.0)

def _moe(h, w_r, b_r, w_in, b_in, w_out, b_out):
    bsz, seq, d = h.shape
    n_tok = bsz * seq
    n_slot = n_tok * TOP_K
    hf = h.reshape(n_tok, d)
    logits = hf @ w_r + b_r
    top_val, top_idx = lax.top_k(logits, TOP_K)
    gates = jax.nn.softmax(top_val.astype(jnp.float32), axis=-1).astype(h.dtype)
    flat_e = top_idx.reshape(-1)
    flat_t = jnp.repeat(jnp.arange(n_tok, dtype=jnp.int32), TOP_K)
    flat_g = gates.reshape(-1)
    order = jnp.argsort(flat_e)
    se = flat_e[order]
    counts = jnp.bincount(flat_e, length=N_EXPERTS)
    padded = (counts + EXPERT_BLOCK - 1) // EXPERT_BLOCK * EXPERT_BLOCK
    ustart = jnp.cumsum(counts) - counts
    pend = jnp.cumsum(padded)
    pstart = pend - padded
    dest = pstart[se] + jnp.arange(n_slot) - ustart[se]
    n_pad = n_slot + N_EXPERTS * EXPERT_BLOCK
    n_blk = n_pad // EXPERT_BLOCK
    tok_pad = jnp.zeros((n_pad,), jnp.int32).at[dest].set(flat_t[order])
    g_pad = jnp.zeros((n_pad,), h.dtype).at[dest].set(flat_g[order])
    blk_e = jnp.minimum(jnp.searchsorted(pend, jnp.arange(n_blk) * EXPERT_BLOCK, side='right'),
                        N_EXPERTS - 1)
    xs = hf[tok_pad].reshape(n_blk, EXPERT_BLOCK, d)

    def expert_block(args):
        xb, e = args
        u = xb @ w_in[e] + b_in[e]
        return _clamped_swiglu(u) @ w_out[e] + b_out[e]

    ys = lax.map(expert_block, (xs, blk_e)).reshape(n_pad, d)
    out = jnp.zeros((n_tok, d), h.dtype).at[tok_pad].add(ys * g_pad[:, None])
    return out.reshape(bsz, seq, d)

def setup_inputs(seed: int = 0) -> dict:
    key = jax.random.key(seed)
    ks = jax.random.split(key, 32)
    D, E, F = D_MODEL, N_EXPERTS, D_EXPERT
    nrm = lambda k, shape, s: jax.random.normal(k, shape, jnp.float32) * s
    return {
        "x": nrm(ks[0], (BATCH, SEQ, D), 1.0),
        "c": nrm(ks[1], (BATCH, D), 1.0),
        "w_mod": nrm(ks[2], (DEPTH, D, 6 * D), 0.5 * D ** -0.5),
        "b_mod": nrm(ks[3], (DEPTH, 6 * D), 0.02),
        "norm_mix_g": 1.0 + nrm(ks[4], (DEPTH, D), 0.02),
        "norm_ffn_g": 1.0 + nrm(ks[5], (DEPTH, D), 0.02),
        "attn_w_qkv": nrm(ks[6], (N_ATTN_LAYERS, D, QKV_DIM), D ** -0.5),
        "attn_b_qkv": nrm(ks[7], (N_ATTN_LAYERS, QKV_DIM), 0.02),
        "attn_w_o": nrm(ks[8], (N_ATTN_LAYERS, Q_DIM, D), Q_DIM ** -0.5),
        "attn_b_o": nrm(ks[9], (N_ATTN_LAYERS, D), 0.02),
        "attn_sinks": nrm(ks[10], (N_ATTN_LAYERS, N_Q_HEADS), 0.5),
        "rel_bias_table": nrm(ks[11], (NUM_BUCKETS, N_Q_HEADS), 0.5),
        "conv_w_in": nrm(ks[12], (N_CONV_LAYERS, D, 2 * CONV_CHANNELS), D ** -0.5),
        "conv_b_in": nrm(ks[13], (N_CONV_LAYERS, 2 * CONV_CHANNELS), 0.02),
        "conv_w_dw": nrm(ks[14], (N_CONV_LAYERS, CONV_WIDTH, CONV_CHANNELS), CONV_WIDTH ** -0.5),
        "conv_b_dw": nrm(ks[15], (N_CONV_LAYERS, CONV_CHANNELS), 0.02),
        "conv_ln_g": 1.0 + nrm(ks[16], (N_CONV_LAYERS, CONV_CHANNELS), 0.02),
        "conv_ln_b": nrm(ks[17], (N_CONV_LAYERS, CONV_CHANNELS), 0.02),
        "conv_w_out": nrm(ks[18], (N_CONV_LAYERS, CONV_CHANNELS, D), CONV_CHANNELS ** -0.5),
        "conv_b_out": nrm(ks[19], (N_CONV_LAYERS, D), 0.02),
        "router_w": nrm(ks[20], (DEPTH, D, E), D ** -0.5),
        "router_b": nrm(ks[21], (DEPTH, E), 0.01),
        "moe_w_in": nrm(ks[22], (DEPTH, E, D, 2 * F), D ** -0.5),
        "moe_b_in": nrm(ks[23], (DEPTH, E, 2 * F), 0.02),
        "moe_w_out": nrm(ks[24], (DEPTH, E, F, D), F ** -0.5),
        "moe_b_out": nrm(ks[25], (DEPTH, E, D), 0.02),
        "final_norm_g": 1.0 + nrm(ks[26], (D,), 0.02),
    }

def reference(x, c, w_mod, b_mod, norm_mix_g, norm_ffn_g, attn_w_qkv, attn_b_qkv, attn_w_o, attn_b_o,
              attn_sinks, rel_bias_table, conv_w_in, conv_b_in, conv_w_dw, conv_b_dw, conv_ln_g, conv_ln_b,
              conv_w_out, conv_b_out, router_w, router_b, moe_w_in, moe_b_in, moe_w_out, moe_b_out,
              final_norm_g):
    rel_bias = _rel_bias(rel_bias_table)
    c_act = jax.nn.silu(c)
    for i in range(DEPTH):
        mod = c_act @ w_mod[i] + b_mod[i]
        sh_m, sc_m, g_m, sh_f, sc_f, g_f = jnp.split(mod, 6, axis=-1)
        h = _rmsnorm(x, norm_mix_g[i]) * (1.0 + sc_m[:, None]) + sh_m[:, None]
        j = i // N_MIXERS
        if i % N_MIXERS == 0:
            m = _sliding_window_attention(h, attn_w_qkv[j], attn_b_qkv[j], attn_w_o[j], attn_b_o[j],
                                          attn_sinks[j], rel_bias)
        else:
            m = _conformer_conv(h, conv_w_in[j], conv_b_in[j], conv_w_dw[j], conv_b_dw[j],
                                conv_ln_g[j], conv_ln_b[j], conv_w_out[j], conv_b_out[j])
        x = x + g_m[:, None] * m
        h = _rmsnorm(x, norm_ffn_g[i]) * (1.0 + sc_f[:, None]) + sh_f[:, None]
        x = x + g_f[:, None] * _moe(h, router_w[i], router_b[i], moe_w_in[i], moe_b_in[i],
                                     moe_w_out[i], moe_b_out[i])
    return _rmsnorm(x, final_norm_g)


_drawn_inputs = setup_inputs


def setup_inputs(seed=0):
    import zlib

    import numpy as np

    out = dict(_drawn_inputs(seed))
    spreads = {}
    factors = {'norm_mix_g': 8.0,
     'norm_ffn_g': 3.404,
     'attn_b_qkv': 6.055,
     'attn_b_o': 5.728,
     'attn_sinks': 59.876,
     'router_b': 21.902,
     'moe_b_in': 8.0,
     'moe_b_out': 41.676,
     'final_norm_g': 7.717}
    for name, (base, spread) in spreads.items():
        noise = np.random.default_rng([zlib.crc32(name.encode()), seed]).standard_normal(out[name].shape)
        drawn = base * np.exp(spread * noise) if base else spread * noise
        out[name] = __import__('jax').numpy.asarray(drawn.astype(out[name].dtype))
    for name, factor in factors.items():
        out[name] = (out[name] * factor).astype(out[name].dtype)
    return out
```

```python
import numpy as np
import concourse.bass as bass
from concourse import mybir
from contextlib import ExitStack

P = 128
D = 1024
SEQ = 1024
KT = D // P
TT = SEQ // P
HD = 64
NQ, NKV, GRP = 16, 4, 4
QKV = 1536
NBUCKET = 32
E = 32
TOPK = 4
F = 1024
EPS = 1e-5
NEG = -1e30
UNITS = TT * NKV
RROW = 3 * P
ITEM = 256
NITEM = SEQ * TOPK // ITEM + E
WIDTHS = (128, 160, 192, 256)
PIECE = 4096
NPIECE = 6
FIELDS = 5
MCOLS = 512
NMOD = 6 * D // MCOLS

V_BMOD, V_GMIX, V_GFFN, V_BQKV, V_BO, V_N = 0, 48, 56, 64, 76, 84


def program(nc, x, c, w_mod, vecs, w_qkv, w_o, sinks, rel_table, router_w, router_b,
            moe_w_in, moe_b, moe_w_out, final_g, bucket_rows, window_fill, out):
    f32 = mybir.dt.float32
    i32 = mybir.dt.int32
    u32 = mybir.dt.uint32
    ALU = mybir.AluOpType
    ACT = mybir.ActivationFunctionType
    AX = mybir.AxisListType

    ctx = ExitStack()
    with ctx:
        def sb(name, shape, dt=f32):
            return ctx.enter_context(nc.sbuf_tensor(name, shape, dt))

        def sem(name):
            return ctx.enter_context(nc.semaphore(name))

        bias_rows_d = nc.dram_tensor("bias_rows_d", [NQ, P, RROW], f32).ap()
        xn_d = nc.dram_tensor("xn_d", [SEQ, D], f32).ap()
        list_d = nc.dram_tensor("list_d", [E * SEQ, 1], u32).ap()
        items_d = nc.dram_tensor("items_d", [NITEM + 1, FIELDS], i32).ap()
        y_d = nc.dram_tensor("y_d", [SEQ * TOPK + ITEM, D], f32).ap()

        ring = sb("ring", [P, NPIECE * PIECE])
        xr = sb("xr", [P, TT, D])
        U = sb("U", [P, 18432])

        def piece(p):
            return ring[:, p * PIECE:(p + 1) * PIECE]

        wqkv = ring[:, 0:3 * PIECE].rearrange("p (k n) -> p k n", k=KT)
        hT = ring[:, 3 * PIECE:5 * PIECE].rearrange("p (k n) -> p k n", k=KT)
        attnT = hT
        wo = ring[:, 0:2 * PIECE].rearrange("p (k n) -> p k n", k=KT)
        scores = ring[:, 2 * PIECE:2 * PIECE + 2048].rearrange("p (b h n) -> p b h n", b=2, h=GRP)
        probsT = ring[:, 5 * PIECE:5 * PIECE + 2048].rearrange("p (b n) -> p b n", b=2)
        heads = ring[:, 5 * PIECE + 2048:5 * PIECE + 2560].rearrange("p (b n) -> p b n", b=2)
        xn2 = ring[:, 2 * PIECE:2 * PIECE + 2048].rearrange("p (b n) -> p b n", b=2)
        junk2 = ring[:, 2 * PIECE + 2048:2 * PIECE + 3072]
        gated = ring[:, 2 * PIECE + 3072:3 * PIECE]
        h2T = ring[:, 5 * PIECE:5 * PIECE + 2048].rearrange("p (b k n) -> p b k n", b=2, k=KT)
        mod_stage = [U[:, 0:PIECE], U[:, PIECE:2 * PIECE], piece(5)]

        qT = U[:, 0:8192].rearrange("p (m n) -> p m n", m=KT)
        kT = U[:, 8192:12288].rearrange("p (g n) -> p g n", g=NKV)
        vv = U[:, 12288:14336].rearrange("p (t n) -> p t n", t=TT)
        relT = U[:, 14336:18432].rearrange("p (h n) -> p h n", h=NQ)
        junk1 = U[:, 8192:9216]
        xn1 = U[:, 9216:11264].rearrange("p (b n) -> p b n", b=2)
        rowsR = U[0:NQ, 11264:11648]
        bucketR = U[0:NBUCKET, 11648:12032]
        fillR = U[0:NQ, 12032:12416]
        gmB = U[:, 0:1024]
        gboB = U[:, 1024:2048]
        diag = U[:, 2048:2304].rearrange("p (b n) -> p b n", b=2)
        xg = U[:, 4096:6144].rearrange("p (b n) -> p b n", b=2)
        xT = U[:, 6144:8192].rearrange("p (k n) -> p k n", k=KT)
        actT = U[:, 0:2048].rearrange("p (k n) -> p k n", k=KT)
        yT = U[:, 2048:4096].rearrange("p (k n) -> p k n", k=KT)
        ysb = U[:, 8192:10240].rearrange("p (b n) -> p b n", b=2)
        gbuf = U[:, 10240:10752].rearrange("p (b n) -> p b n", b=2)
        lbuf = [U[:, 10752:11008], U[:, 11008:11264], U[:, 14080:14336]]
        sbuf_ = U[:, 11264:11776].rearrange("p (b n) -> p b n", b=2)
        gsbuf = U[:, 11776:12288].rearrange("p (b n) -> p b n", b=2)
        fgB = U[:, 12288:13312]
        biasT = U[:, 13312:14080].rearrange("p (e n) -> p e n", e=E)
        onehot = U[:, 14336:15360].rearrange("p (t j e) -> p t j e", t=TT, j=TOPK)
        ohpos = U[:, 15360:16384].rearrange("p (t j e) -> p t j e", t=TT, j=TOPK)
        mask = U[:, 16384:16640].rearrange("p (t e) -> p t e", t=TT)
        macc = U[:, 17940:18196].rearrange("p (t e) -> p t e", t=TT)
        brow = U[:, 16900:17668].rearrange("p (r n) -> p r n", r=6)
        meta = U[:, 18236:18236 + FIELDS]
        metai = U[:, 18250:18250 + FIELDS].bitcast(i32)
        items = U[0:1, 17668:17668 + FIELDS * (NITEM + 1)].bitcast(i32)
        nrow = items[:, 3:4]
        idx = U[:, 17914:17916].bitcast(u32)
        bias_now = U[:, 17916:17940]
        lo = U[:, 0:512].rearrange("p (r e) -> p r e", r=16)
        gates = U[:, 18196:18228].rearrange("p (t j) -> p t j", t=TT)
        gsum = U[:, 18228:18236]
        ydest = U[:, 18268:18300].bitcast(u32)
        ydf = U[:, 18300:18332]
        yg = ring[:, 0:8192].rearrange("p (b j n) -> p b j n", b=2, j=TOPK)
        outb = ring[:, 8192:10240].rearrange("p (b n) -> p b n", b=2)
        junk3 = ring[:, 10240:11264]

        ident = sb("ident", [P, P])
        ones = sb("ones", [P, P])
        tri = sb("tri", [P, P])
        vecr = sb("vecr", [V_N, P])
        vecT = sb("vecT", [P, V_N])
        modT = sb("modT", [P, 48])
        cT = sb("cT", [P, KT])
        cS = sb("cS", [P, KT])
        cA = sb("cA", [P, KT])
        eps = sb("eps", [P, 1])
        Am = sb("Am", [P, KT])
        Af = sb("Af", [P, KT])
        gbo = sb("gbo", [P, KT])
        bq8 = sb("bq8", [P, KT])
        table = sb("table", [NBUCKET, NQ])
        sinkB = sb("sinkB", [P, NQ])
        nsink = sb("nsink", [P, NQ])
        ss = sb("ss", [P, 3 * TT])
        sd = sb("sd", [P, 3 * TT])
        rstd = sb("rstd", [P, 3 * TT])
        bvB = sb("bvB", [P, 256])
        brB = sb("brB", [P, E])
        wr = sb("wr", [P, KT, E])
        zeros = U[:, 12416:12672].bitcast(u32)
        tok_i = sb("tok_i", [P, TT], i32)
        e_i = sb("e_i", [P, E], i32)
        e_f = sb("e_f", [P, E])
        e1k = sb("e1k", [P, E])
        p_i = sb("p_i", [P, 1], i32)
        p_f = sb("p_f", [P, 1])
        top8 = sb("top8", [P, TT, 8])
        idx8 = sb("idx8", [P, 8], u32)
        idxf = sb("idxf", [P, 8])
        lg = sb("lg", [P, E])
        pos = sb("pos", [P, E])
        destf = sb("destf", [P, TT * TOPK])
        dest = sb("dest", [P, TT * TOPK], u32)
        negm = sb("negm", [P, 2, GRP])
        dsk = sb("dsk", [P, 2, GRP])
        mx = sb("mx", [P, 2, GRP])
        rs = sb("rs", [P, 2, GRP])
        es = sb("es", [P, 2, GRP])
        den = sb("den", [P, 2, GRP])
        rec = sb("rec", [P, 2, GRP])

        ps = ctx.enter_context(nc.psum_tensor("ps", [P, 8 * 512], f32))

        def bank(b, n=1):
            return ps[:, 512 * b:512 * (b + n)]

        s_c = sem("c_loaded"); s_vec = sem("vecs_loaded")
        s_x = [sem(f"x_loaded{t}") for t in range(TT)]
        s_small = sem("small_loaded")
        s_mod = [sem(f"mod_piece_loaded{b}") for b in range(3)]
        s_modmm = sem("mod_product"); s_modT = sem("modT_ready")
        s_wqkv = sem("wqkv_loaded"); s_const = sem("constants_ready"); s_p = sem("pool_chain")
        s_v = sem("dve_chain"); s_a = sem("act_chain")
        s_cs = sem("sigmoid_c"); s_ca = sem("silu_c")
        s_vT = sem("vecs_transposed"); s_vecT = sem("vecT_ready")
        s_sq = sem("squares_done"); s_sd = sem("std_done"); s_rstd = sem("rstd_ready")
        s_xn = sem("xn_ready"); s_xt = sem("x_transposed"); s_hta = sem("hT_by_act"); s_htv = sem("hT_by_dve")
        s_coef = sem("norm_coefs")
        s_R = sem("bias_row_product"); s_Rs = sem("bias_rows_ready"); s_Rd = sem("bias_rows_stored")
        s_T = sem("bias_tables_loaded")
        s_qkv = sem("qkv_product"); s_qa = sem("qkv_by_act"); s_qv = sem("qkv_by_dve"); s_kd = sem("k_doubled")
        s_wo = sem("wo_loaded")
        s_sc = sem("scores_product"); s_sadd = sem("scores_biased"); s_nm = sem("negmax_ready")
        s_exp = sem("probs_ready"); s_ptr = sem("probs_transposed"); s_pta = sem("probsT_by_act")
        s_ptv = sem("probsT_by_dve"); s_pv = sem("pv_product"); s_o = sem("heads_ready")
        s_ot = sem("heads_transposed"); s_at = sem("attnT_ready")
        s_dg = sem("diag_ready"); s_bc = sem("broadcast_product"); s_gB = sem("gates_broadcast"); s_xb = sem("x_plus_bias")
        s_op = sem("o_product"); s_x1 = sem("x1_ready"); s_sq2 = sem("std2_ready"); s_xn2 = sem("xn2_ready")
        s_xnd = [sem(f"xn_stored{b}") for b in range(2)]; s_x2 = sem("xn2_transposed"); s_h2a = sem("h2T_by_act"); s_h2v = sem("h2T_by_dve")
        s_lg = sem("logits_product"); s_mask = sem("mask_ready"); s_rank = sem("rank_product")
        s_dest = sem("places_ready"); s_sct = sem("ids_scattered"); s_zero = sem("list_zeroed")
        s_cnt = sem("counts_product"); s_meta = sem("items_ready"); s_itd = sem("items_stored"); s_row = sem("items_row_loaded")
        s_brow = sem("moe_biases_loaded"); s_bt = sem("moe_biases_transposed"); s_bT = sem("biasT_ready")
        s_late = sem("late_small_loaded")
        s_lv = sem("gate_logits"); s_ge = sem("gate_exps")
        s_wl = [sem(f"piece_loaded{p}") for p in range(NPIECE)]
        s_idx = sem("ids_loaded"); s_g = sem("rows_gathered"); s_xtp = sem("rows_transposed"); s_xT = sem("xT_ready")
        s_mm = sem("step_product"); s_je = sem("up_evacuated"); s_gr = sem("glu_ready"); s_sg = sem("sigmoid_ready")
        s_act = sem("act_ready"); s_me = sem("down_evacuated"); s_ytp = sem("y_transposed"); s_ye = sem("y_evacuated")
        s_yst = sem("y_stored"); s_go = sem("gather_goes"); s_clear = sem("y_buffer_cleared")
        s_yd = sem("y_places_ready"); s_yg = [sem(f"y_gathered{b}") for b in range(2)]
        s_acc = sem("rows_added"); s_sq3 = sem("std3_ready"); s_ob = sem("out_ready"); s_st = [sem(f"out_stored{b}") for b in range(2)]

        groups = [("k", m, h) for m in range(2) for h in range(2)] + [("v", t, 0) for t in range(TT)] \
            + [("q", m, h) for m in range(KT) for h in range(2)]
        by_act = [n for n, g in enumerate(groups) if g[0] != "v"]
        by_dve = [n for n, g in enumerate(groups) if g[0] == "v"]

        def wait_group_evacuated(eng, n):
            if groups[n][0] == "v":
                eng.wait_ge(s_qv, by_dve.index(n) + 1)
            else:
                eng.wait_ge(s_qa, by_act.index(n) + 1)

        def head_at(place):
            return 2 * (place % 2) + place // 2

        w_in_v = moe_w_in.rearrange("e (k p) (s q n) -> e q p k s n", p=P, s=2, n=256)
        w_out_v = moe_w_out.rearrange("e (k p) (q n) -> e q p k n", p=P, n=512)

        def load_pieces_of(eng, e, p):
            if p < 4:
                dst = piece(p).rearrange("p (k s n) -> p k s n", k=KT, s=2)
                for s in range(2):
                    last = eng.dma_start(dst[:, :, s, :], w_in_v[e, p, :, :, s, :] if isinstance(e, int)
                                         else w_in_v[bass.ds(e, 1), p, :, :, s, :].rearrange("o p k n -> (o p) k n"))
                    last.then_inc(s_wl[p], 16)
            else:
                dst = piece(p).rearrange("p (k n) -> p k n", k=KT)
                src = w_out_v[e, p - 4] if isinstance(e, int) else \
                    w_out_v[bass.ds(e, 1), p - 4].rearrange("o p k n -> (o p) k n")
                eng.dma_start(dst, src).then_inc(s_wl[p], 16)

        steps_to = [2, 4, 6, 8, 12, 16]

        block = ctx.enter_context(nc.Block())

        @block.sync
        def _(sp):
            sp.dma_start(cT[:, :], c.rearrange("o (p t) -> p (o t)", p=P)).then_inc(s_c, 16)
            sp.dma_start(vecr[:, :], vecs).then_inc(s_vec, 16)
            for t in range(TT):
                sp.dma_start(xr[:, t, :], x[t * P:(t + 1) * P, :]).then_inc(s_x[t], 16)
            mod_v = w_mod.rearrange("(p t) (q n) -> q p t n", p=P, n=MCOLS)

            def load_mod(n):
                b = n if n < 3 else (0 if n == 3 else 2)
                sp.dma_start(mod_stage[b].rearrange("p (t n) -> p t n", t=KT), mod_v[n]).then_inc(s_mod[b], 16)

            for n in range(3):
                load_mod(n)
            sp.wait_ge(s_modmm, 1)
            load_mod(3)
            wq_v = w_qkv.rearrange("(k p) n -> p k n", p=P)
            for k in range(KT):
                sp.dma_start(wqkv[:, k, :], wq_v[:, k, :]).then_inc(s_wqkv, 16)
            sp.wait_ge(s_Rs, 1)
            sp.dma_start(bias_rows_d, rowsR.rearrange("h (o n) -> h o n", o=1).to_broadcast([NQ, P, RROW])).then_inc(s_Rd, 16)
            sp.wait_ge(s_Rd, 16)
            for h in range(NQ):
                g, r = h // GRP, h % GRP
                place = g * GRP + (r % 2) * 2 + r // 2
                src = bass.AP(tensor=bias_rows_d.tensor, offset=h * P * RROW + P - 1, ap=[[RROW - 1, P], [1, 2 * P]])
                sp.dma_start(relT[:, place, :], src).then_inc(s_T, 16)
            for n in range(4, NMOD):
                if n == 4:
                    sp.wait_ge(s_modmm, 3)
                else:
                    sp.wait_ge(s_modmm, n)
                load_mod(n)
                if n == 5:
                    sp.wait_ge(s_qa, 4)
                    for g in range(NKV):
                        here = slice(64 * (g % 2), 64 * (g % 2) + 64)
                        there = slice(64 - 64 * (g % 2), 128 - 64 * (g % 2))
                        sp.dma_start(kT[there, g, :], kT[here, g, :]).then_inc(s_kd, 16)
            sp.wait_ge(s_qkv, len(groups))
            wo_v = w_o.rearrange("(k p) n -> p k n", p=P)
            for k in range(KT):
                sp.dma_start(wo[:, k, :], wo_v[:, k, :]).then_inc(s_wo, 16)
            sp.wait_ge(s_pv, UNITS)
            sp.wait_ge(s_sadd, UNITS)
            sp.dma_start(brow[:, :, :], moe_b.rearrange("(r p) n -> p r n", p=P)).then_inc(s_brow, 16)
            sp.dma_start(fgB, final_g.partition_broadcast(P)).then_inc(s_late, 16)
            for t in range(TT):
                sp.wait_ge(s_xn2, t + 1)
                sp.dma_start(xn_d[t * P:(t + 1) * P, :], xn2[:, t % 2, :]).then_inc(s_xnd[t % 2], 16)
            sp.wait_ge(s_op, TT)
            load_pieces_of(sp, 0, 0)
            load_pieces_of(sp, 0, 1)
            sp.wait_ge(s_meta, 1)
            sp.dma_start(items_d, metai[0:NITEM + 1, :]).then_inc(s_itd, 16)
            sp.wait_ge(s_itd, 16)
            sp.dma_start(items, items_d.rearrange("(o i) n -> o (i n)", o=1)).then_inc(s_row, 16)
            for b in range(2):
                sp.wait_ge(s_xnd[b], TT // 2 * 16)
            load_pieces_of(sp, 0, 2)
            for p in (3, 4, 5):
                load_pieces_of(sp, 0, p)
            sp.wait_ge(s_row, 16)
            n_items = sp.value_load(nrow, min_val=1, max_val=NITEM)
            with sp.Fori(1, NITEM) as i:
                with sp.If(i < n_items):
                    e = sp.value_load(items[:, bass.ds(i * FIELDS, 1)], min_val=0, max_val=E - 1)
                    for p in range(NPIECE):
                        sp.wait_ge(s_mm, (i - 1) * 16 + steps_to[p])
                        load_pieces_of(sp, e, p)
            for t in range(TT):
                sp.wait_ge(s_ob, t + 1)
                sp.dma_start(out[t * P:(t + 1) * P, :], outb[:, t % 2, :]).then_inc(s_st[t % 2], 16)
            sp.wait_ge(s_st[0], TT // 2 * 16)
            sp.wait_ge(s_st[1], TT // 2 * 16)

        @block.gpsimd
        def _(pool):
            pc = [0]

            def link(ins):
                pc[0] += 1
                ins.then_inc(s_p, 1)
                pool.wait_ge(s_p, pc[0])

            pool.memset(eps[:, :], EPS)
            pool.memset(ones[:, :], 1.0)
            pool.memset(ident[:, :], 0.0)
            link(pool.memset(zeros, 0))
            pool.dma_start(list_d.rearrange("(p n) o -> p (n o)", p=P), zeros).then_inc(s_zero, 16)
            pool.affine_select(out=ident[:, :], in_=ident[:, :], compare_op=ALU.not_equal, fill=1.0,
                               base=0, pattern=[[-1, P]], channel_multiplier=1)
            pool.affine_select(out=tri[:, :], in_=ones[:, :], compare_op=ALU.is_gt, fill=0.0,
                               base=0, pattern=[[1, P]], channel_multiplier=-1)
            pool.iota(tok_i[:, :], pattern=[[P, TT]], base=0, channel_multiplier=1)
            pool.iota(e_i[:, :], pattern=[[1, E]], base=0, channel_multiplier=0)
            pool.iota(p_i[:, :], pattern=[[0, 1]], base=0, channel_multiplier=1).then_inc(s_const, 1)
            pool.dma_start(table[:, :], rel_table).then_inc(s_small, 16)
            pool.dma_start(bucketR, bucket_rows).then_inc(s_small, 16)
            pool.dma_start(fillR, window_fill).then_inc(s_small, 16)
            pool.dma_start(sinkB[:, :], sinks.partition_broadcast(P)).then_inc(s_small, 16)
            pool.dma_start(bvB[:, :], vecs.rearrange("r n -> (r n)")[(V_BQKV + 10) * P:(V_BQKV + 12) * P]
                           .partition_broadcast(P)).then_inc(s_small, 16)
            pool.dma_start(brB[:, :], router_b.partition_broadcast(P)).then_inc(s_small, 16)
            pool.dma_start(wr[:, :, :], router_w.rearrange("(k p) n -> p k n", p=P)).then_inc(s_small, 16)
            pool.wait_ge(s_rstd, 1)
            for t in range(TT):
                if t >= 2:
                    pool.wait_ge(s_xt, 2 * (t - 1))
                pool.tensor_scalar(xn1[:, t % 2, :], xr[:, t, :], rstd[:, t:t + 1], None, ALU.mult)\
                    .then_inc(s_xn, 1)
            pool.wait_ge(s_gB, 1)
            for t in range(TT):
                pool.tensor_tensor(out=xr[:, t, :], in0=xr[:, t, :], in1=gboB, op=ALU.add).then_inc(s_xb, 1)
            pool.wait_ge(s_zero, 16)
            for t in range(TT):
                pool.wait_ge(s_dest, t + 1)
                for j in range(TOPK):
                    n = t * TOPK + j
                    pool.indirect_dma_start(out=list_d, out_offset=bass.IndirectOffsetOnAxis(ap=dest[:, n:n + 1], axis=0),
                                            in_=tok_i[:, t:t + 1].bitcast(u32), in_offset=None).then_inc(s_sct, 16)
            pool.wait_ge(s_sct, TT * TOPK * 16)
            for b in range(2):
                pool.wait_ge(s_xnd[b], TT // 2 * 16)

            def load_ids(start):
                with nc.allow_non_contiguous_dma(reason="one id per partition"):
                    src = list_d[bass.ds(start, ITEM), :].rearrange("(b p) o -> p (b o)", p=P)
                    pool.dma_start(idx, src).then_inc(s_idx, 16)

            def gather_rows():
                for b in range(2):
                    pool.indirect_dma_start(out=xg[:, b, :], out_offset=None, in_=xn_d,
                                            in_offset=bass.IndirectOffsetOnAxis(ap=idx[:, b:b + 1], axis=0))\
                        .then_inc(s_g, 16)

            pool.wait_ge(s_clear, 1)
            pool.dma_start(y_d[0:1, 0:P], ysb[0:1, 0, 0:P]).then_inc(s_yst, 16)
            load_ids(0)
            pool.wait_ge(s_idx, 16)
            gather_rows()
            pool.wait_ge(s_row, 16)
            n_items = pool.value_load(nrow, min_val=1, max_val=NITEM)
            with pool.Fori(0, NITEM) as i:
                with pool.If(i < n_items):
                    start = pool.value_load(items[:, bass.ds(i * FIELDS + FIELDS + 1, 1)], min_val=0, max_val=E * SEQ - ITEM)
                    width = pool.value_load(items[:, bass.ds(i * FIELDS + 2, 1)], min_val=0, max_val=3)
                    pool.wait_ge(s_g, (i + 1) * 32)
                    load_ids(start)
                    pool.wait_ge(s_idx, (i + 2) * 16)
                    pool.wait_ge(s_xtp, (i + 1) * 4)
                    pool.sem_inc(s_go, 1)
                    gather_rows()
                    first = pool.value_load(items[:, bass.ds(i * FIELDS + 4, 1)], min_val=0, max_val=SEQ * TOPK)
                    row = y_d[bass.ds(first, ITEM), :].rearrange("(b p) n -> p b n", p=P)
                    with pool.If(width == 0):
                        pool.wait_ge(s_ye, (i + 1) * 4)
                        pool.dma_start(row[:, 0, :], ysb[:, 0, :]).then_inc(s_yst, 16)
                    with pool.If(width > 0):
                        pool.wait_ge(s_ye, (i + 1) * 4)
                        pool.dma_start(row, ysb[:, :, :]).then_inc(s_yst, 16)
            pool.wait_ge(s_yst, (n_items + 1) * 16)
            pool.sem_inc(s_go, 1)
            pool.wait_ge(s_yd, 1)
            for t in range(TT):
                if t >= 2:
                    pool.wait_ge(s_acc, t - 1)
                for j in range(TOPK):
                    n = t * TOPK + j
                    pool.indirect_dma_start(out=yg[:, t % 2, j, :], out_offset=None, in_=y_d[0:SEQ * TOPK, :],
                                            in_offset=bass.IndirectOffsetOnAxis(ap=ydest[:, n:n + 1], axis=0))\
                        .then_inc(s_yg[t % 2], 16)

        @block.scalar
        def _(act):
            ac = [0]

            def link(ins):
                ac[0] += 1
                ins.then_inc(s_a, 1)
                act.wait_ge(s_a, ac[0])

            act.wait_ge(s_c, 16)
            act.activation(cS[:, :], cT[:, :], ACT.Sigmoid).then_inc(s_cs, 1)
            for t in range(TT):
                act.wait_ge(s_x[t], 16)
                if t == TT - 1:
                    act.wait_ge(s_const, 1)
                link(act.activation(junk1, xr[:, t, :], ACT.Square, accum_out=ss[:, t:t + 1]))
            act.activation(sd[:, 0:TT], ss[:, 0:TT], ACT.Sqrt, scale=1.0 / D, bias=eps[:, 0:1]).then_inc(s_sd, 1)
            act.wait_ge(s_vT, 1)
            act.activation(vecT[:, :], bank(6)[:, 0:V_N], ACT.Copy).then_inc(s_vecT, 1)
            act.wait_ge(s_coef, 1)
            for t in range(TT):
                act.wait_ge(s_xt, 2 * t + 1)
                for k in range(4):
                    last = act.activation(hT[:, k, t * P:(t + 1) * P], bank(2 * t % 4)[:, k * P:(k + 1) * P],
                                          ACT.Identity, scale=Am[:, k:k + 1], bias=modT[:, k:k + 1])
                last.then_inc(s_hta, 1)
            for n in by_act:
                kind, m, h = groups[n]
                act.wait_ge(s_qkv, n + 1)
                cols = slice(h * 512, h * 512 + 512)
                if kind == "k":
                    for z in range(2):
                        part = slice(64 * z, 64 * z + 64)
                        last = act.activation(kT[part, 2 * m + z, cols], bank(n % 4)[part, :], ACT.Identity,
                                              bias=vecT[part, V_BQKV + 8 + m:V_BQKV + 9 + m])
                else:
                    last = act.activation(qT[:, m, cols], bank(n % 4), ACT.Identity, scale=0.125, bias=bq8[:, m:m + 1])
                last.then_inc(s_qa, 1)

            def probs_evacuate(u):
                b = u // NKV
                act.wait_ge(s_ptr, u + 1)
                if u >= 2:
                    act.wait_ge(s_pv, u - 1)
                src = bank(4).rearrange("p (h k n) -> p h k n", h=2, k=2)
                dst = probsT[:, u % 2, 0:512].rearrange("p (h k n) -> p h k n", h=2, k=2)
                lo_k = 0 if b else 1
                act.activation(dst[:, :, lo_k:, :], src[:, :, lo_k:, :], ACT.Copy).then_inc(s_pta, 1)

            def heads_evacuate(u):
                b, g = u // NKV, u % NKV
                act.wait_ge(s_ot, u + 1)
                act.activation(attnT[:, 2 * g:2 * g + 2, b * P:(b + 1) * P],
                               bank(7)[:, 0:256].rearrange("p (m n) -> p m n", m=2), ACT.Copy).then_inc(s_at, 1)

            for u in range(UNITS + 3):
                if u < UNITS:
                    z = 0 if u // NKV else P
                    act.wait_ge(s_nm, u + 1)
                    for r in range(GRP):
                        act.activation(scores[:, u % 2, r, z:], scores[:, u % 2, r, z:], ACT.Exp,
                                       bias=negm[:, u % 2, r:r + 1], accum_out=rs[:, u % 2, r:r + 1])
                    act.activation(es[:, u % 2, :], dsk[:, u % 2, :], ACT.Exp).then_inc(s_exp, 1)
                if 1 <= u <= UNITS:
                    probs_evacuate(u - 1)
                if u >= 3:
                    heads_evacuate(u - 3)

            def h2_evacuate(t):
                act.wait_ge(s_x2, 2 * t + 1)
                if t >= 2:
                    act.wait_ge(s_lg, t - 1)
                for k in range(4):
                    last = act.activation(h2T[:, t % 2, k, :], bank(4)[:, k * P:(k + 1) * P], ACT.Identity,
                                          scale=Af[:, k:k + 1], bias=modT[:, 24 + k:25 + k])
                last.then_inc(s_h2a, 1)

            for t in range(TT + 1):
                if t < TT:
                    act.wait_ge(s_x1, t + 1)
                    link(act.activation(junk2, xr[:, t, :], ACT.Square, accum_out=ss[:, TT + t:TT + t + 1]))
                    act.activation(sd[:, TT + t:TT + t + 1], ss[:, TT + t:TT + t + 1], ACT.Sqrt, scale=1.0 / D,
                                   bias=eps[:, 0:1]).then_inc(s_sq2, 1)
                if t >= 1:
                    h2_evacuate(t - 1)
            act.wait_ge(s_lv, 1)
            act.activation(gates[:, :, :], gates[:, :, :], ACT.Exp).then_inc(s_ge, 1)

            def rows_evacuate(ks, done):
                for k in ks:
                    if k % 2 == 0:
                        act.wait_ge(s_xtp, done + k // 2 + 1)
                    act.activation(xT[:, k, :], bank(4 + k // 2 % 2)[:, (k % 2) * 256:(k % 2) * 256 + 256], ACT.Identity,
                                   scale=Af[:, k:k + 1], bias=modT[:, 24 + k:25 + k]).then_inc(s_xT, 1)

            rows_evacuate(range(KT), 0)
            act.wait_ge(s_row, 16)
            n_items = act.value_load(nrow, min_val=1, max_val=NITEM)

            def item(i, n):
                for j in range(8):
                    act.wait_ge(s_gr, i * 8 + j + 1)
                    act.activation(sbuf_[:, j % 2, 0:n], gbuf[:, j % 2, 0:n], ACT.Sigmoid, scale=1.702)\
                        .then_inc(s_sg, 1)

                def down(m):
                    act.wait_ge(s_mm, i * 16 + 8 + m + 1)
                    act.activation(yT[:, m, 0:n], bank(m % 4)[:, 0:n], ACT.Identity, scale=modT[:, 40 + m:41 + m],
                                   bias=bias_now[:, 16 + m:17 + m]).then_inc(s_me, 1)

                act.wait_ge(s_mm, i * 16 + 8)
                rows_evacuate(range(4), i * 4 + 4)
                down(0)
                down(1)
                rows_evacuate(range(4, 8), i * 4 + 4)
                for m in range(2, 8):
                    down(m)

            with act.Fori(0, NITEM) as i:
                with act.If(i < n_items):
                    width = act.value_load(items[:, bass.ds(i * FIELDS + 2, 1)], min_val=0, max_val=3)
                    for w, n in enumerate(WIDTHS):
                        with act.If(width == w):
                            item(i, n)
            for t in range(TT):
                act.wait_ge(s_acc, t + 1)
                last = act.activation(junk3, xr[:, t, :], ACT.Square, accum_out=ss[:, 16 + t:17 + t])
                link(last)
                act.activation(sd[:, 16 + t:17 + t], ss[:, 16 + t:17 + t], ACT.Sqrt, scale=1.0 / D,
                               bias=eps[:, 0:1]).then_inc(s_sq3, 1)

        @block.vector
        def _(dve):
            vc = [0]

            def link(ins):
                vc[0] += 1
                ins.then_inc(s_v, 1)
                dve.wait_ge(s_v, vc[0])

            dve.wait_ge(s_cs, 1)
            dve.tensor_tensor(out=cA[:, :], in0=cT[:, :], in1=cS[:, :], op=ALU.mult).then_inc(s_ca, 1)
            dve.wait_ge(s_const, 1)
            dve.tensor_copy(p_f[:, :], p_i[:, :])
            link(dve.tensor_copy(e_f[:, :], e_i[:, :]))
            dve.tensor_scalar(e1k[:, :], e_f[:, :], float(SEQ), None, ALU.mult)
            dve.wait_ge(s_small, 112)
            dve.tensor_scalar(nsink[:, :].rearrange("p (g a r) -> p g a r", g=NKV, a=2),
                              sinkB[:, :].rearrange("p (g r a) -> p g a r", g=NKV, a=2), -1.0, None, ALU.mult)
            dve.wait_ge(s_R, 1)
            dve.tensor_tensor(out=rowsR, in0=bank(5)[0:NQ, 0:RROW], in1=fillR, op=ALU.add).then_inc(s_Rs, 1)
            dve.wait_ge(s_sd, 1)
            dve.reciprocal(rstd[:, 0:TT], sd[:, 0:TT]).then_inc(s_rstd, 1)
            dve.wait_ge(s_vecT, 1)
            dve.tensor_scalar(bq8[:, :], vecT[:, V_BQKV:V_BQKV + 8], 0.125, None, ALU.mult)

            def mod_evacuate(n):
                dve.wait_ge(s_modmm, n + 1)
                dve.tensor_tensor(out=modT[:, 4 * n:4 * n + 4], in0=bank(6 + n % 2)[:, 4 * n:4 * n + 4],
                                  in1=vecT[:, 4 * n:4 * n + 4], op=ALU.add).then_inc(s_modT, 1)
                dve.wait_ge(s_modT, n + 1)

            for n in range(4):
                mod_evacuate(n)
            link(dve.scalar_tensor_tensor(out=Am[:, :], in0=modT[:, 8:16], scalar=1.0,
                                          in1=vecT[:, V_GMIX:V_GMIX + 8], op0=ALU.add, op1=ALU.mult))
            dve.engine_nop().then_inc(s_coef, 1)
            for t in range(TT):
                dve.wait_ge(s_xt, 2 * t + 2)
                for k in range(4, 8):
                    last = dve.tensor_scalar(hT[:, k, t * P:(t + 1) * P], bank((2 * t + 1) % 4)[:, (k - 4) * P:(k - 3) * P],
                                             Am[:, k:k + 1], modT[:, k:k + 1], ALU.mult, ALU.add)
                last.then_inc(s_htv, 1)
            dve.wait_ge(s_zero, 16)
            for n, (kind, t, _) in enumerate(groups):
                if kind == "v":
                    dve.wait_ge(s_qkv, n + 1)
                    dve.tensor_tensor(out=vv[:, t, :], in0=bank(n % 4)[:, 0:256], in1=bvB[:, :], op=ALU.add)\
                        .then_inc(s_qv, 1)
                if n % 3 == 2 and 4 + n // 3 < NMOD:
                    mod_evacuate(4 + n // 3)
            dve.scalar_tensor_tensor(out=Af[:, :], in0=modT[:, 32:40], scalar=1.0,
                                     in1=vecT[:, V_GFFN:V_GFFN + 8], op0=ALU.add, op1=ALU.mult)
            link(dve.tensor_tensor(out=gbo[:, :], in0=modT[:, 16:24], in1=vecT[:, V_BO:V_BO + 8], op=ALU.mult))

            dve.wait_ge(s_T, NQ * 16)

            def scores_in(u):
                b, g = u // NKV, u % NKV
                z = 0 if b else P
                dve.wait_ge(s_sc, u + 1)
                if u >= 2:
                    dve.wait_ge(s_ptr, u - 1)
                s = scores[:, u % 2, :, z:]
                src = bank(2 * (u % 2), 2).rearrange("p (h n) -> p h n", h=GRP)[:, :, z:]
                vc[0] += 1
                dve.tensor_tensor(out=s, in0=src, in1=relT[:, g * GRP:(g + 1) * GRP, z:], op=ALU.add).then_inc(s_sadd, 1)
                vc[0] -= 1
                dve.wait_ge(s_sadd, u + 1)
                link(dve.tensor_reduce(out=mx[:, u % 2, :], in_=s, axis=AX.X, op=ALU.max))
                link(dve.scalar_tensor_tensor(out=negm[:, u % 2, :], in0=mx[:, u % 2, :], scalar=-1.0,
                                              in1=nsink[:, g * GRP:(g + 1) * GRP], op0=ALU.mult, op1=ALU.min))
                dve.tensor_tensor(out=dsk[:, u % 2, :], in0=negm[:, u % 2, :], in1=nsink[:, g * GRP:(g + 1) * GRP],
                                  op=ALU.subtract).then_inc(s_nm, 1)

            def probs_out(u):
                lo_k = 0 if u // NKV else 1
                dve.wait_ge(s_ptr, u + 1)
                if u >= 2:
                    dve.wait_ge(s_pv, u - 1)
                src = bank(5).rearrange("p (h k n) -> p h k n", h=2, k=2)
                dst = probsT[:, u % 2, 512:1024].rearrange("p (h k n) -> p h k n", h=2, k=2)
                dve.tensor_copy(dst[:, :, lo_k:, :], src[:, :, lo_k:, :]).then_inc(s_ptv, 1)
                link(dve.tensor_tensor(out=den[:, u % 2, :], in0=rs[:, u % 2, :], in1=es[:, u % 2, :], op=ALU.add))
                link(dve.reciprocal(rec[:, u % 2, :], den[:, u % 2, :]))

            def heads_out(u):
                dve.wait_ge(s_pv, u + 1)
                if u >= 2:
                    dve.wait_ge(s_ot, u - 1)
                src = bank(6)[:, 0:256].rearrange("p (a r d) -> p a r d", a=2, r=2)
                dst = heads[:, u % 2, :].rearrange("p (r a d) -> p a r d", a=2, r=2)
                by = rec[:, u % 2, :].rearrange("p (a r o) -> p a r o", a=2, o=1).to_broadcast([P, 2, 2, HD])
                dve.tensor_tensor(out=dst, in0=src, in1=by, op=ALU.mult).then_inc(s_o, 1)

            for u in range(UNITS + 2):
                if u < UNITS:
                    scores_in(u)
                if u >= 2:
                    heads_out(u - 2)
                if 1 <= u <= UNITS:
                    probs_out(u - 1)

            for n in range(2 * KT):
                k = n % KT
                col = modT[:, 16 + k:17 + k] if n < KT else gbo[:, k:k + 1]
                if n >= 2:
                    dve.wait_ge(s_bc, n - 1)
                elif n == 0:
                    dve.wait_ge(s_sc, UNITS)
                dve.tensor_scalar(diag[:, n % 2, :], ident[:, :], col, None, ALU.mult).then_inc(s_dg, 1)
            dve.wait_ge(s_bc, 2 * KT)
            dve.tensor_copy(gmB, bank(0, 2))
            dve.tensor_copy(gboB, bank(2, 2)).then_inc(s_gB, 1)
            dve.memset(ysb[:, :, :], 0.0).then_inc(s_clear, 1)

            def residual(t):
                dve.wait_ge(s_op, t + 1)
                link(dve.tensor_tensor(out=gated, in0=bank(2 * (t % 2), 2), in1=gmB, op=ALU.mult))
                dve.wait_ge(s_xb, t + 1)
                dve.tensor_tensor(out=xr[:, t, :], in0=xr[:, t, :], in1=gated, op=ALU.add).then_inc(s_x1, 1)

            def norm2(t):
                dve.wait_ge(s_sq2, t + 1)
                link(dve.reciprocal(rstd[:, TT + t:TT + t + 1], sd[:, TT + t:TT + t + 1]))
                if t >= 2:
                    dve.wait_ge(s_x2, 2 * (t - 1))
                    dve.wait_ge(s_xnd[t % 2], 16 * (t // 2))
                dve.tensor_scalar(xn2[:, t % 2, :], xr[:, t, :], rstd[:, TT + t:TT + t + 1], None, ALU.mult)\
                    .then_inc(s_xn2, 1)

            def h2_out(t):
                dve.wait_ge(s_x2, 2 * t + 2)
                if t >= 2:
                    dve.wait_ge(s_lg, t - 1)
                for k in range(4, 8):
                    last = dve.tensor_scalar(h2T[:, t % 2, k, :], bank(5)[:, (k - 4) * P:(k - 3) * P],
                                             Af[:, k:k + 1], modT[:, 24 + k:25 + k], ALU.mult, ALU.add)
                last.then_inc(s_h2v, 1)

            def choose(t):
                dve.wait_ge(s_lg, t + 1)
                link(dve.tensor_tensor(out=lg[:, :], in0=bank(6)[:, 0:E], in1=brB[:, :], op=ALU.add))
                link(dve.max(out=top8[:, t, :], in_=lg[:, :]))
                link(dve.max_index(out=idx8[:, :], in_max=top8[:, t, :], in_values=lg[:, :]))
                link(dve.tensor_copy(idxf[:, :], idx8[:, :]))
                link(dve.tensor_tensor(out=onehot[:, t, :, :],
                                       in0=idxf[:, 0:TOPK].rearrange("p (j o) -> p j o", o=1).to_broadcast([P, TOPK, E]),
                                       in1=e_f[:, :].rearrange("p (o e) -> p o e", o=1).to_broadcast([P, TOPK, E]),
                                       op=ALU.is_equal))
                dve.tensor_reduce(out=mask[:, t, :], in_=onehot[:, t, :, :].rearrange("p j e -> p e j"), axis=AX.X,
                                  op=ALU.add).then_inc(s_mask, 1)
                dve.wait_ge(s_mask, t + 1)
                if t:
                    link(dve.tensor_tensor(out=macc[:, t, :], in0=macc[:, t - 1, :], in1=mask[:, t, :], op=ALU.add))
                else:
                    link(dve.tensor_copy(macc[:, 0, :], mask[:, 0, :]))
                dve.wait_ge(s_rank, t + 1)
                link(dve.tensor_tensor(out=pos[:, :], in0=bank(7)[:, 0:E], in1=e1k[:, :], op=ALU.add))
                link(dve.tensor_tensor(out=ohpos[:, t, :, :], in0=onehot[:, t, :, :],
                                       in1=pos[:, :].rearrange("p (o e) -> p o e", o=1).to_broadcast([P, TOPK, E]),
                                       op=ALU.mult))
                link(dve.tensor_reduce(out=destf[:, t * TOPK:(t + 1) * TOPK], in_=ohpos[:, t, :, :], axis=AX.X, op=ALU.add))
                dve.tensor_copy(dest[:, t * TOPK:(t + 1) * TOPK], destf[:, t * TOPK:(t + 1) * TOPK]).then_inc(s_dest, 1)

            for t in range(TT + 2):
                if t < TT:
                    residual(t)
                    norm2(t)
                if 1 <= t <= TT:
                    h2_out(t - 1)
                if t >= 2:
                    choose(t - 2)

            dve.wait_ge(s_cnt, 1)
            nb, cnt = lo[:, 0, :], lo[:, 1, :]
            link(dve.tensor_copy(cnt, bank(6)[:, 64:64 + E]))
            link(dve.tensor_scalar(nb, cnt, 0.0, None, ALU.is_gt))
            for over in range(ITEM, SEQ, ITEM):
                link(dve.scalar_tensor_tensor(out=nb, in0=cnt, scalar=float(over), in1=nb, op0=ALU.is_gt, op1=ALU.add))
            link(dve.tensor_scalar(nb[:, 0:1], nb[:, 0:1], 1.0, None, ALU.max))
            link(dve.tensor_copy(lo[:, 2:4, :], lo[:, 0:2, :]))
            cur = 2
            for step in (1, 2, 4, 8, 16):
                nxt = 6 - cur
                dve.tensor_copy(lo[:, nxt:nxt + 2, 0:step], lo[:, cur:cur + 2, 0:step])
                link(dve.tensor_tensor(out=lo[:, nxt:nxt + 2, step:], in0=lo[:, cur:cur + 2, step:],
                                       in1=lo[:, cur:cur + 2, 0:E - step], op=ALU.add))
                cur = nxt
            ends = lo[:, cur, :]
            starts, ystarts = lo[:, 6, :], lo[:, 7, :]
            link(dve.tensor_tensor(out=lo[:, 6:8, :], in0=lo[:, cur:cur + 2, :], in1=lo[:, 0:2, :], op=ALU.subtract))
            le, rel, mine, junk = lo[:, 8, :], lo[:, 9, :], lo[:, 10, :], lo[:, 11, :]
            dve.tensor_scalar(le, starts, p_f[:, 0:1], None, ALU.is_le)
            link(dve.tensor_scalar(rel, starts, -1.0, p_f[:, 0:1], ALU.mult, ALU.add))
            link(dve.scalar_tensor_tensor(out=mine, in0=ends, scalar=p_f[:, 0:1], in1=le, op0=ALU.is_gt, op1=ALU.mult))
            dve.scalar_tensor_tensor(out=lo[:, 12, :], in0=rel, scalar=float(ITEM), in1=e1k[:, :], op0=ALU.mult, op1=ALU.add)
            dve.scalar_tensor_tensor(out=lo[:, 13, :], in0=rel, scalar=float(ITEM), in1=ystarts, op0=ALU.mult, op1=ALU.add)
            link(dve.scalar_tensor_tensor(out=lo[:, 14, :], in0=rel, scalar=-float(ITEM), in1=cnt, op0=ALU.mult, op1=ALU.add))
            for col, src in ((0, e_f[:, :]), (1, lo[:, 12, :]), (4, lo[:, 13, :]), (2, lo[:, 14, :])):
                link(dve.scalar_tensor_tensor(out=junk, in0=mine, scalar=1.0, in1=src, op0=ALU.mult, op1=ALU.mult,
                                              accum_out=meta[:, col:col + 1]))
            link(dve.tensor_copy(junk[:, 0:1], meta[:, 2:3]))
            link(dve.tensor_scalar(meta[:, 2:3], junk[:, 0:1], float(WIDTHS[0]), None, ALU.is_gt))
            for w in WIDTHS[1:-1]:
                link(dve.scalar_tensor_tensor(out=meta[:, 2:3], in0=junk[:, 0:1], scalar=float(w), in1=meta[:, 2:3],
                                              op0=ALU.is_gt, op1=ALU.add))
            link(dve.tensor_copy(meta[:, 3:4], ends[:, E - 1:E]))
            dve.tensor_copy(metai, meta).then_inc(s_meta, 1)
            link(dve.tensor_tensor(out=gates[:, :, :], in0=top8[:, :, 0:TOPK],
                                   in1=top8[:, :, 0:1].to_broadcast([P, TT, TOPK]), op=ALU.subtract))
            dve.engine_nop().then_inc(s_lv, 1)
            dve.wait_ge(s_bt, 1)
            bsrc = bank(2, 2)[:, 0:768].rearrange("p (e n) -> p e n", e=E)
            dve.tensor_copy(biasT[:, :, 0:8], bsrc[:, :, 0:8])
            dve.tensor_scalar(biasT[:, :, 8:16], bsrc[:, :, 8:16], 1.0, None, ALU.add)
            link(dve.tensor_tensor(out=biasT[:, :, 16:24], in0=bsrc[:, :, 16:24],
                                   in1=modT[:, 40:48].rearrange("p (o n) -> p o n", o=1).to_broadcast([P, E, 8]), op=ALU.mult))
            dve.engine_nop().then_inc(s_bT, 1)
            val = lo[:, 15, :]
            link(dve.tensor_tensor(out=val, in0=ystarts, in1=e1k[:, :], op=ALU.subtract))
            link(dve.tensor_tensor(out=ohpos[:, :, :, :].rearrange("p t j e -> p (t j) e"),
                                   in0=onehot[:, :, :, :].rearrange("p t j e -> p (t j) e"),
                                   in1=val.rearrange("p (o e) -> p o e", o=1).to_broadcast([P, TT * TOPK, E]), op=ALU.mult))
            link(dve.tensor_reduce(out=ydf, in_=ohpos[:, :, :, :].rearrange("p t j e -> p (t j) e"), axis=AX.X, op=ALU.add))
            link(dve.tensor_tensor(out=ydf, in0=ydf, in1=destf[:, :], op=ALU.add))
            dve.tensor_copy(ydest, ydf).then_inc(s_yd, 1)
            dve.wait_ge(s_ge, 1)
            link(dve.tensor_reduce(out=gsum, in_=gates[:, :, :], axis=AX.X, op=ALU.add))
            link(dve.reciprocal(gsum, gsum))
            link(dve.tensor_tensor(out=gates[:, :, :], in0=gates[:, :, :],
                                   in1=gsum.rearrange("p (t o) -> p t o", o=1).to_broadcast([P, TT, TOPK]), op=ALU.mult))

            dve.wait_ge(s_row, 16)
            n_items = dve.value_load(nrow, min_val=1, max_val=NITEM)
            before = vc[0]

            def item(i, e, n, wide):
                k = [0]
                per_item = 1 + 8

                def link_i(ins):
                    k[0] += 1
                    ins.then_inc(s_v, 1)
                    dve.wait_ge(s_v, i * per_item + (before + k[0]))

                link_i(dve.tensor_copy(bias_now, biasT[:, bass.ds(e, 1), :].rearrange("p o n -> p (o n)")))

                def up(j):
                    dve.wait_ge(s_mm, i * 16 + j + 1)
                    dve.tensor_scalar(gbuf[:, j % 2, 0:n], bank(j % 4)[:, 0:n], bias_now[:, j:j + 1], 7.0,
                                      ALU.add, ALU.min).then_inc(s_gr, 1)
                    dve.tensor_scalar(lbuf[j % 3][:, 0:n], bank(j % 4)[:, 256:256 + n], bias_now[:, 8 + j:9 + j], -6.0,
                                      ALU.add, ALU.max).then_inc(s_je, 1)

                def activate(j):
                    dve.wait_ge(s_sg, i * 8 + j + 1)
                    link_i(dve.tensor_tensor(out=gsbuf[:, j % 2, 0:n], in0=gbuf[:, j % 2, 0:n],
                                             in1=sbuf_[:, j % 2, 0:n], op=ALU.mult))
                    dve.scalar_tensor_tensor(out=actT[:, j, 0:n], in0=lbuf[j % 3][:, 0:n], scalar=8.0,
                                             in1=gsbuf[:, j % 2, 0:n], op0=ALU.min, op1=ALU.mult).then_inc(s_act, 1)

                for j in range(9):
                    if j < 8:
                        up(j)
                    if j >= 1:
                        activate(j - 1)
                dve.wait_ge(s_yst, i * 16 + 16)
                for r in range(4 if wide else 2):
                    b, h = r // 2, r % 2
                    rows = n - b * P if b else P
                    all_ = 4 if not wide and r == 1 else r + 1
                    dve.wait_ge(s_ytp, i * 4 + all_)
                    dve.tensor_copy(ysb[0:rows, b, h * 512:h * 512 + 512], bank((4 if b else 6) + h)[0:rows, :])\
                        .then_inc(s_ye, 3 if not wide and r == 1 else 1)

            with dve.Fori(0, NITEM) as i:
                with dve.If(i < n_items):
                    e = dve.value_load(items[:, bass.ds(i * FIELDS, 1)], min_val=0, max_val=E - 1)
                    width = dve.value_load(items[:, bass.ds(i * FIELDS + 2, 1)], min_val=0, max_val=3)
                    for w, n in enumerate(WIDTHS):
                        with dve.If(width == w):
                            item(i, e, n, w > 0)

            dve.wait_ge(s_late, 16)
            s_done = s_dg
            dc = [2 * KT]

            def link_last(ins):
                dc[0] += 1
                ins.then_inc(s_done, 1)
                dve.wait_ge(s_done, dc[0])

            def finish(t):
                dve.wait_ge(s_sq3, t + 1)
                link_last(dve.reciprocal(rstd[:, 16 + t:17 + t], sd[:, 16 + t:17 + t]))
                if t >= 2:
                    dve.wait_ge(s_st[t % 2], 16 * (t // 2))
                dve.scalar_tensor_tensor(out=outb[:, t % 2, :], in0=xr[:, t, :], scalar=rstd[:, 16 + t:17 + t],
                                         in1=fgB, op0=ALU.mult, op1=ALU.mult).then_inc(s_ob, 1)

            for t in range(TT + 1):
                if t < TT:
                    dve.wait_ge(s_yg[t % 2], 64 * (t // 2 + 1))
                    for j in range(TOPK):
                        ins = dve.scalar_tensor_tensor(out=xr[:, t, :], in0=yg[:, t % 2, j, :], scalar=gates[:, t, j:j + 1],
                                                       in1=xr[:, t, :], op0=ALU.mult, op1=ALU.add)
                        if j < TOPK - 1:
                            link_last(ins)
                        else:
                            ins.then_inc(s_acc, 1)
                if t >= 1:
                    finish(t - 1)

        @block.tensor
        def _(pe):
            pe.wait_ge(s_const, 1)
            pe.wait_ge(s_vec, 16)
            pe.transpose(bank(6)[:, 0:V_N], vecr[:, :], ident[0:V_N, 0:V_N]).then_inc(s_vT, 1)
            pe.wait_ge(s_small, 112)
            pe.matmul(bank(5)[0:NQ, 0:RROW], table[:, :], bucketR, start=True, stop=True).then_inc(s_R, 1)
            pe.wait_ge(s_ca, 1)

            def mod_products(n):
                b = n if n < 3 else (0 if n == 3 else 2)
                pe.wait_ge(s_mod[b], 16 * (1 if n < 3 else 2 if n == 3 else n - 2))
                w = mod_stage[b].rearrange("p (t n) -> p t n", t=KT)
                if n == 0:
                    pe.wait_ge(s_vecT, 1)
                elif n >= 2:
                    pe.wait_ge(s_modT, n - 1)
                for q in range(4):
                    for t in range(KT):
                        last = pe.matmul(bank(6 + n % 2)[:, 4 * n + q:4 * n + q + 1], w[:, t, q * P:(q + 1) * P], cA[:, t:t + 1],
                                         start=(t == 0), stop=(t == KT - 1))
                last.then_inc(s_modmm, 1)

            for n in range(4):
                mod_products(n)
            for t in range(TT):
                pe.wait_ge(s_xn, t + 1)
                for h in range(2):
                    n = 2 * t + h
                    if n >= 4:
                        pe.wait_ge(s_htv if h else s_hta, (n - 4) // 2 + 1)
                    for k in range(4):
                        last = pe.transpose(bank(n % 4)[:, k * P:(k + 1) * P],
                                            xn1[:, t % 2, (4 * h + k) * P:(4 * h + k + 1) * P], ident[:, :])
                    last.then_inc(s_xt, 1)
            pe.wait_ge(s_wqkv, KT * 16)
            pe.wait_ge(s_hta, TT)
            pe.wait_ge(s_htv, TT)
            for n, (kind, m, h) in enumerate(groups):
                if n >= 4:
                    wait_group_evacuated(pe, n - 4)
                for k in range(KT):
                    if kind == "v":
                        last = pe.matmul(bank(n % 4)[:, 0:256], hT[:, k, m * P:(m + 1) * P], wqkv[:, k, 1280:1536],
                                         start=(k == 0), stop=(k == KT - 1))
                    else:
                        col = m * P if kind == "q" else D + m * P
                        last = pe.matmul(bank(n % 4), wqkv[:, k, col:col + P], hT[:, k, h * 512:h * 512 + 512],
                                         start=(k == 0), stop=(k == KT - 1))
                last.then_inc(s_qkv, 1)
                if n % 3 == 2 and 4 + n // 3 < NMOD:
                    mod_products(4 + n // 3)

            def scores_product(u):
                b, g = u // NKV, u % NKV
                if u >= 2:
                    pe.wait_ge(s_sadd, u - 1)
                for place in range(GRP):
                    r = head_at(place)
                    part = slice(64 * (r % 2), 64 * (r % 2) + 64)
                    lo_c, lo_k = (0, (b - 1) * P) if b else (P, 0)
                    last = pe.matmul(bank(2 * (u % 2), 2)[:, place * 256 + lo_c:place * 256 + 256],
                                     qT[part, 2 * g + r // 2, b * P:(b + 1) * P], kT[part, g, lo_k:(b + 1) * P],
                                     start=True, stop=True)
                last.then_inc(s_sc, 1)

            def probs_transpose(u):
                pe.wait_ge(s_exp, u + 1)
                if u >= 1:
                    pe.wait_ge(s_pta, u)
                    pe.wait_ge(s_ptv, u)
                for place in range(GRP):
                    for kb in range(0 if u // NKV else 1, 2):
                        last = pe.transpose(bank(4, 2)[:, (place * 2 + kb) * P:(place * 2 + kb + 1) * P],
                                            scores[:, u % 2, place, kb * P:(kb + 1) * P], ident[:, :])
                last.then_inc(s_ptr, 1)

            def pv_product(u):
                b, g = u // NKV, u % NKV
                pe.wait_ge(s_pta, u + 1)
                pe.wait_ge(s_ptv, u + 1)
                if u >= 1:
                    pe.wait_ge(s_o, u)
                for place in range(GRP):
                    first = 0 if b else 1
                    for kb in range(first, 2):
                        last = pe.matmul(bank(6)[:, place * HD:(place + 1) * HD],
                                         probsT[:, u % 2, (place * 2 + kb) * P:(place * 2 + kb + 1) * P],
                                         vv[:, b - 1 + kb, g * HD:(g + 1) * HD], start=(kb == first), stop=(kb == 1))
                last.then_inc(s_pv, 1)

            def heads_transpose(u):
                pe.wait_ge(s_o, u + 1)
                if u >= 1:
                    pe.wait_ge(s_at, u)
                for z in range(2):
                    last = pe.transpose(bank(7)[:, z * P:(z + 1) * P], heads[:, u % 2, z * P:(z + 1) * P], ident[:, :])
                last.then_inc(s_ot, 1)

            pe.wait_ge(s_qa, len(by_act))
            pe.wait_ge(s_qv, len(by_dve))
            pe.wait_ge(s_kd, NKV * 16)
            scores_product(0)
            scores_product(1)
            for u in range(UNITS + 2):
                if u < UNITS:
                    probs_transpose(u)
                if u + 2 < UNITS:
                    scores_product(u + 2)
                if 1 <= u <= UNITS:
                    pv_product(u - 1)
                if u >= 2:
                    heads_transpose(u - 2)

            for n in range(2 * KT):
                pe.wait_ge(s_dg, n + 1)
                pe.matmul(bank(0, 4)[:, n * P:(n + 1) * P], ones[:, :], diag[:, n % 2, :], start=True, stop=True)\
                    .then_inc(s_bc, 1)
            pe.wait_ge(s_wo, KT * 16)
            pe.wait_ge(s_at, UNITS)
            pe.wait_ge(s_gB, 1)

            def o_product(t):
                if t >= 2:
                    pe.wait_ge(s_x1, t - 1)
                for h in range(2):
                    for k in range(KT):
                        last = pe.matmul(bank(2 * (t % 2) + h), attnT[:, k, t * P:(t + 1) * P],
                                         wo[:, k, h * 512:h * 512 + 512], start=(k == 0), stop=(k == KT - 1))
                last.then_inc(s_op, 1)

            def xn2_transpose(t):
                pe.wait_ge(s_xn2, t + 1)
                for h in range(2):
                    if t >= 1:
                        pe.wait_ge(s_h2v if h else s_h2a, t)
                    for k in range(4):
                        last = pe.transpose(bank(4 + h)[:, k * P:(k + 1) * P],
                                            xn2[:, t % 2, (4 * h + k) * P:(4 * h + k + 1) * P], ident[:, :])
                    last.then_inc(s_x2, 1)

            def logits(t):
                pe.wait_ge(s_h2a, t + 1)
                pe.wait_ge(s_h2v, t + 1)
                if t >= 1:
                    pe.wait_ge(s_mask, t)
                for k in range(KT):
                    last = pe.matmul(bank(6)[:, 0:E], h2T[:, t % 2, k, :], wr[:, k, :], start=(k == 0), stop=(k == KT - 1))
                last.then_inc(s_lg, 1)

            def ranks(t):
                pe.wait_ge(s_mask, t + 1)
                if t >= 1:
                    pe.wait_ge(s_dest, t)
                last = pe.matmul(bank(7)[:, 0:E], tri[:, :], mask[:, t, :], start=True, stop=(t == 0))
                if t:
                    last = pe.matmul(bank(7)[:, 0:E], ones[:, :], macc[:, t - 1, :], start=False, stop=True)
                last.then_inc(s_rank, 1)

            for t in range(TT + 3):
                if t < TT:
                    o_product(t)
                if 1 <= t <= TT:
                    xn2_transpose(t - 1)
                if 2 <= t <= TT + 1:
                    logits(t - 2)
                if t >= 3:
                    ranks(t - 3)
            pe.wait_ge(s_dest, TT)
            pe.matmul(bank(6)[:, 64:64 + E], ones[:, :], macc[:, TT - 1, :], start=True, stop=True).then_inc(s_cnt, 1)
            pe.wait_ge(s_brow, 16)
            for r in range(6):
                last = pe.transpose(bank(2, 2)[:, r * P:(r + 1) * P], brow[:, r, :], ident[:, :])
            last.then_inc(s_bt, 1)

            def rows_transpose(pairs, i):
                for kp in pairs:
                    if kp >= 2:
                        pe.wait_ge(s_xT, i * 8 + 2 * (kp - 1))
                    for k in range(2):
                        for b in range(2):
                            last = pe.transpose(bank(4 + kp % 2)[:, k * 256 + b * P:k * 256 + (b + 1) * P],
                                                xg[:, b, (2 * kp + k) * P:(2 * kp + k + 1) * P], ident[:, :])
                    last.then_inc(s_xtp, 1)

            pe.wait_ge(s_g, 32)
            pe.wait_ge(s_h2a, TT)
            rows_transpose(range(4), 0)
            pe.wait_ge(s_bT, 1)
            pe.wait_ge(s_row, 16)
            n_items = pe.value_load(nrow, min_val=1, max_val=NITEM)

            def item(i, n, wide):
                for j in range(8):
                    if j % 2 == 0:
                        pe.wait_ge(s_wl[j // 2], i * 32 + 32)
                    if j >= 4:
                        pe.wait_ge(s_je, i * 8 + j - 3)
                    if j == 0:
                        pe.wait_ge(s_xT, i * 8 + 8)
                    w = piece(j // 2).rearrange("p (k s n) -> p k s n", k=KT, s=2)
                    for s in range(2):
                        for k in range(KT):
                            last = pe.matmul(bank(j % 4)[:, s * 256:s * 256 + n], w[:, k, s, (j % 2) * P:(j % 2 + 1) * P],
                                             xT[:, k, 0:n], start=(k == 0), stop=(k == KT - 1))
                    last.then_inc(s_mm, 1)
                pe.wait_ge(s_g, i * 32 + 64)
                rows_transpose(range(2), i + 1)
                for m in range(8):
                    if m % 4 == 0:
                        pe.wait_ge(s_wl[4 + m // 4], i * 16 + 16)
                    if m < 4:
                        pe.wait_ge(s_je, i * 8 + m + 5)
                    else:
                        pe.wait_ge(s_me, i * 8 + m - 3)
                    w = piece(4 + m // 4).rearrange("p (k n) -> p k n", k=KT)
                    for k in range(KT):
                        if m == 0:
                            pe.wait_ge(s_act, i * 8 + k + 1)
                        last = pe.matmul(bank(m % 4)[:, 0:n], w[:, k, (m % 4) * P:(m % 4 + 1) * P], actT[:, k, 0:n],
                                         start=(k == 0), stop=(k == KT - 1))
                    last.then_inc(s_mm, 1)
                    if m == 1:
                        rows_transpose(range(2, 4), i + 1)
                for r in range(4 if wide else 2):
                    b, h = r // 2, r % 2
                    rows = n - b * P if b else P
                    for m in range(4 * h, 4 * h + 4):
                        if b == 0:
                            pe.wait_ge(s_me, i * 8 + m + 1)
                        last = pe.transpose(bank((4 if b else 6) + h)[0:rows, (m % 4) * P:(m % 4 + 1) * P],
                                            yT[:, m, b * P:b * P + rows], ident[:, :])
                    last.then_inc(s_ytp, 3 if not wide and r == 1 else 1)

            with pe.Fori(0, NITEM) as i:
                with pe.If(i < n_items):
                    width = pe.value_load(items[:, bass.ds(i * FIELDS + 2, 1)], min_val=0, max_val=3)
                    for w, n in enumerate(WIDTHS):
                        with pe.If(width == w):
                            item(i, n, w > 0)


def relative_constants():
    r = np.arange(RROW)
    dist = 2 * P - 1 - r
    n = np.maximum(dist, 0)
    exact = NBUCKET // 2
    large = exact + (np.log(np.maximum(n, 1) / exact) / np.log(P / exact) * (NBUCKET - exact) + 1e-9).astype(np.int64)
    bucket = np.where(n < exact, n, np.minimum(large, NBUCKET - 1))
    inside = (dist >= 0) & (dist < P)
    rows = ((bucket[None, :] == np.arange(NBUCKET)[:, None]) & inside[None, :]).astype(np.float32)
    fill = np.where(inside, np.float32(0), np.float32(NEG)).astype(np.float32)
    return rows, np.broadcast_to(fill, (NQ, RROW)).copy()


def kernel(x, c, w_mod, b_mod, norm_mix_g, norm_ffn_g, attn_w_qkv, attn_b_qkv, attn_w_o, attn_b_o,
           attn_sinks, rel_bias_table, conv_w_in, conv_b_in, conv_w_dw, conv_b_dw, conv_ln_g, conv_ln_b,
           conv_w_out, conv_b_out, router_w, router_b, moe_w_in, moe_b_in, moe_w_out, moe_b_out,
           final_norm_g):
    import concourse.bacc as _bacc
    from concourse.bass_utils import run_bass_kernel_spmd as _run

    def rows(*vectors):
        return np.concatenate([np.asarray(v).reshape(-1, P) for v in vectors], axis=0)

    bucket_rows, window_fill = relative_constants()
    ins = {
        "x": np.asarray(x)[0], "c": np.asarray(c), "w_mod": np.asarray(w_mod)[0],
        "vecs": rows(b_mod, norm_mix_g, norm_ffn_g, attn_b_qkv, attn_b_o),
        "w_qkv": np.asarray(attn_w_qkv)[0], "w_o": np.asarray(attn_w_o)[0],
        "sinks": np.asarray(attn_sinks)[0], "rel_table": np.asarray(rel_bias_table),
        "router_w": np.asarray(router_w)[0], "router_b": np.asarray(router_b)[0],
        "moe_w_in": np.asarray(moe_w_in)[0],
        "moe_b": np.concatenate([np.asarray(moe_b_in)[0].reshape(E, 16, P), np.asarray(moe_b_out)[0].reshape(E, 8, P)],
                                axis=1).reshape(E * 24, P),
        "moe_w_out": np.asarray(moe_w_out)[0], "final_g": np.asarray(final_norm_g),
        "bucket_rows": bucket_rows, "window_fill": window_fill,
    }
    nc = _bacc.Bacc("TRN2", target_bir_lowering=False, num_devices=1)
    arrays, args = {}, []
    for name, a in ins.items():
        a = np.ascontiguousarray(a)
        arrays[f"in_{name}"] = a
        args.append(nc.dram_tensor(f"in_{name}", a.shape, mybir.dt.from_np(a.dtype), kind="ExternalInput").ap())
    args.append(nc.dram_tensor("out_0", (SEQ, D), mybir.dt.float32, kind="ExternalOutput").ap())
    program(nc, *args)
    r = _run(nc, [arrays], core_ids=[0])
    return r.results[0]["out_0"].reshape(1, SEQ, D)
```

```python
import numpy as np
import concourse.bass as bass
from concourse import mybir
from contextlib import ExitStack

P = 128
D = 1024
SEQ = 1024
KT = D // P
TT = SEQ // P
HD = 64
NQ, NKV, GRP = 16, 4, 4
QKV = 1536
NBUCKET = 32
E = 32
TOPK = 4
F = 1024
EPS = 1e-5
NEG = -1e30
UNITS = TT * NKV
RROW = 3 * P
ITEM = 256
NITEM = (SEQ * TOPK + E * (ITEM - 1)) // ITEM
WIDTHS = (128, 136, 144, 152, 160, 168, 176, 184, 192, 208, 224, 256)
NARROW = sum(w <= P for w in WIDTHS)
PIECE = 4096
NPIECE = 6
FIELDS = 5
NYG = 4
MCOLS = 512
NMOD = 6 * D // MCOLS

V_BMOD, V_GMIX, V_GFFN, V_BQKV, V_BO, V_N = 0, 48, 56, 64, 76, 84


def by_width(eng, width, body, first=0, end=None):
    end = len(WIDTHS) if end is None else end
    if end - first == 1:
        body(first)
        return
    mid = (first + end) // 2
    with eng.If(width < mid):
        by_width(eng, width, body, first, mid)
    with eng.Else():
        by_width(eng, width, body, mid, end)


def program(nc, x, c, w_mod, vecs, w_qkv, w_o, sinks, rel_table, router_w, router_b,
            moe_w_in, moe_b, moe_w_out, final_g, bucket_rows, window_fill, out):
    f32 = mybir.dt.float32
    i32 = mybir.dt.int32
    u32 = mybir.dt.uint32
    ALU = mybir.AluOpType
    ACT = mybir.ActivationFunctionType
    AX = mybir.AxisListType

    ctx = ExitStack()
    with ctx:
        def sb(name, shape, dt=f32):
            return ctx.enter_context(nc.sbuf_tensor(name, shape, dt))

        def sem(name):
            return ctx.enter_context(nc.semaphore(name))

        bias_rows_d = nc.dram_tensor("bias_rows_d", [NQ, P, RROW], f32).ap()
        xn_d = nc.dram_tensor("xn_d", [SEQ, D], f32).ap()
        list_d = nc.dram_tensor("list_d", [E * SEQ, 1], u32).ap()
        items_d = nc.dram_tensor("items_d", [NITEM + 1, FIELDS], i32).ap()
        y_d = nc.dram_tensor("y_d", [SEQ * TOPK + ITEM, D], f32).ap()

        ring = sb("ring", [P, NPIECE * PIECE])
        xr = sb("xr", [P, TT, D])
        U = sb("U", [P, 18432])

        def piece(p):
            return ring[:, p * PIECE:(p + 1) * PIECE]

        wq = ring[:, 0:2 * PIECE].rearrange("p (k n) -> p k n", k=KT)
        wkv = piece(2).rearrange("p (k n) -> p k n", k=KT)
        hT = ring[:, 3 * PIECE:5 * PIECE].rearrange("p (k n) -> p k n", k=KT)
        attnT = hT
        wo = wq
        late = 2 * PIECE
        scores = ring[:, late:late + 2048].rearrange("p (b h n) -> p b h n", b=2, h=GRP)
        heads = ring[:, late + 2048:late + 2560].rearrange("p (b n) -> p b n", b=2)
        gated = ring[:, late + 2560:late + 3072]
        junk2 = ring[:, late + 3072:late + 3584].bitcast(mybir.dt.bfloat16)
        mask = ring[:, late + 3584:late + 3840].rearrange("p (t e) -> p t e", t=TT)
        macc = ring[:, late + 3840:late + 4096].rearrange("p (t e) -> p t e", t=TT)
        probsT = ring[:, 5 * PIECE:5 * PIECE + 2048].rearrange("p (b n) -> p b n", b=2)
        gmB = ring[:, 5 * PIECE + 2048:5 * PIECE + 3072]
        gboB = ring[:, 5 * PIECE + 3072:6 * PIECE]
        onehot = gboB.rearrange("p (t j e) -> p t j e", t=TT, j=TOPK)
        stages = [U[:, 0:PIECE], U[:, PIECE:2 * PIECE], piece(5), piece(3)]
        stage_of = [0, 1, 2, 3, 0, 1, 2, 0, 1, 2, 0, 1]
        mod_sum = U[:, 15872:16896].rearrange("p (b n) -> p b n", b=2)

        qT = U[:, 0:8192].rearrange("p (h m n) -> p h m n", h=2, m=KT)
        kT = U[:, 8192:12288].rearrange("p (g n) -> p g n", g=NKV)
        vv = U[:, 12288:14336].rearrange("p (t n) -> p t n", t=TT)
        relT = U[:, 14336:18432].rearrange("p (h n) -> p h n", h=NQ)
        junk1 = U[:, 8192:9216]
        xn1 = ring[:, 0:2 * PIECE].rearrange("p (b n) -> p b n", b=TT)
        rowsR = U[0:NQ, 14336:14720]
        bucketR = U[0:NBUCKET, 14720:15104]
        fillR = U[0:NQ, 15104:15488]
        diag = ring[:, late + 2560:late + 2816].rearrange("p (b n) -> p b n", b=2)
        xn2 = U[:, 0:2048].rearrange("p (b n) -> p b n", b=2)
        h2T = U[:, 2048:4096].rearrange("p (b k n) -> p b k n", b=2, k=KT)
        xg = U[:, 4096:6144].rearrange("p (b n) -> p b n", b=2)
        xT = U[:, 6144:8192].rearrange("p (k n) -> p k n", k=KT)
        actT = U[:, 0:2048].rearrange("p (k n) -> p k n", k=KT)
        yT = U[:, 2048:4096].rearrange("p (k n) -> p k n", k=KT)
        ysb = U[:, 8192:10240].rearrange("p (b n) -> p b n", b=2)
        gbuf = U[:, 10240:10752].rearrange("p (b n) -> p b n", b=2)
        lbuf = [U[:, 10752:11008], U[:, 11008:11264], U[:, 14080:14336]]
        sbuf_ = U[:, 11264:11776].rearrange("p (b n) -> p b n", b=2)
        gsbuf = U[:, 11776:12288].rearrange("p (b n) -> p b n", b=2)
        fgB = U[:, 12288:13312]
        biasT = U[:, 13312:14080].rearrange("p (e n) -> p e n", e=E)
        ohpos = U[:, 15360:16384].rearrange("p (t j e) -> p t j e", t=TT, j=TOPK)
        brow = U[:, 16900:17668].rearrange("p (r n) -> p r n", r=6)
        meta = U[:, 18236:18236 + FIELDS]
        metai = U[:, 18250:18250 + FIELDS].bitcast(i32)
        items = U[0:1, 17668:17668 + FIELDS * (NITEM + 1)].bitcast(i32)
        nrow = items[:, 3:4]
        idx = U[:, 17914:17916].bitcast(u32)
        bias_now = U[:, 17916:17940]
        lo = U[:, 10240:10752].rearrange("p (r e) -> p r e", r=16)
        gates = U[:, 18196:18228].rearrange("p (t j) -> p t j", t=TT)
        gsum = U[:, 18228:18236]
        ydest = U[:, 18268:18300].bitcast(u32)
        ydf = U[:, 18300:18332]
        yg = ring[:, 0:NYG * TOPK * D].rearrange("p (b j n) -> p b j n", b=NYG, j=TOPK)
        outb = ring[:, 16384:18432].rearrange("p (b n) -> p b n", b=2)
        junk3 = ring[:, 18432:19456]

        ident = sb("ident", [P, P])
        ones = sb("ones", [P, P])
        tri = sb("tri", [P, P])
        vecr = sb("vecr", [V_N, P])
        vecT = sb("vecT", [P, V_N])
        modT = sb("modT", [P, 48])
        cT = sb("cT", [P, KT])
        cS = sb("cS", [P, KT])
        cA = sb("cA", [P, KT])
        Am = sb("Am", [P, KT])
        Af = sb("Af", [P, KT])
        gbo = sb("gbo", [P, KT])
        bq8 = sb("bq8", [P, KT])
        table = sb("table", [NBUCKET, NQ])
        sinkB = sb("sinkB", [P, NQ])
        nsink = sb("nsink", [P, NQ])
        ss = sb("ss", [P, 3 * TT])
        var = sb("var", [P, 3 * TT])
        mhalf = sb("mhalf", [P, TT])
        ohp = sb("ohp", [P, TOPK, E])
        rstd = sb("rstd", [P, 3 * TT])
        bvB = sb("bvB", [P, 256])
        brB = sb("brB", [P, E])
        wr = sb("wr", [P, KT, E])
        zeros = U[:, 15488:15744].bitcast(u32)
        tok_i = sb("tok_i", [P, TT], i32)
        e_i = sb("e_i", [P, E], i32)
        e_f = sb("e_f", [P, E])
        e1k = sb("e1k", [P, E])
        p_i = sb("p_i", [P, 1], i32)
        p_f = sb("p_f", [P, 1])
        top8 = sb("top8", [P, TT, 8])
        idx8 = sb("idx8", [P, 8], u32)
        idxf = sb("idxf", [P, 8])
        lg = sb("lg", [P, E])
        pos = sb("pos", [P, E])
        destf = sb("destf", [P, TT * TOPK])
        dest = sb("dest", [P, TT * TOPK], u32)
        negm = sb("negm", [P, 2, GRP])
        dsk = sb("dsk", [P, 2, GRP])
        mx = sb("mx", [P, 2, GRP])
        rs = sb("rs", [P, 2, GRP])
        es = sb("es", [P, 2, GRP])
        den = sb("den", [P, 2, GRP])
        rec = sb("rec", [P, 2, GRP])

        ps = ctx.enter_context(nc.psum_tensor("ps", [P, 8 * 512], f32))

        def bank(b, n=1):
            return ps[:, 512 * b:512 * (b + n)]

        s_c = sem("c_loaded"); s_vec = sem("vecs_loaded")
        s_x = [sem(f"x_loaded{t}") for t in range(TT)]
        s_small = sem("small_loaded")
        s_mod = [sem(f"mod_piece_loaded{b}") for b in range(4)]
        s_msum = sem("mod_summed"); s_modmm = sem("mod_product"); s_modT = sem("modT_ready")
        s_wkv = sem("wkv_loaded"); s_wq = sem("wq_loaded"); s_const = sem("constants_ready"); s_p = sem("pool_chain")
        s_v = sem("dve_chain"); s_a = sem("act_chain")
        s_cs = sem("sigmoid_c"); s_ca = sem("silu_c")
        s_vT = sem("vecs_transposed"); s_vecT = sem("vecT_ready")
        s_sq = sem("squares_done"); s_rstd = sem("rstd_ready")
        s_xn = sem("xn_ready"); s_xt = sem("x_transposed"); s_hta = sem("hT_by_act"); s_htv = sem("hT_by_dve")
        s_coef = sem("norm_coefs")
        s_R = sem("bias_row_product"); s_Rs = sem("bias_rows_ready"); s_Rd = sem("bias_rows_stored")
        s_T = sem("bias_tables_loaded")
        s_qkv = sem("qkv_product"); s_qa = sem("qkv_by_act"); s_qv = sem("qkv_by_dve"); s_kd = sem("k_doubled")
        s_wo = [sem(f"wo_loaded{z}") for z in range(2)]
        s_sc = sem("scores_product"); s_sadd = sem("scores_biased"); s_nm = sem("negmax_ready")
        s_exp = sem("probs_ready"); s_ptr = sem("probs_transposed"); s_pta = sem("probsT_by_act")
        s_ptv = sem("probsT_by_dve"); s_pv = sem("pv_product"); s_o = sem("heads_ready")
        s_ot = sem("heads_transposed"); s_at = sem("attnT_ready")
        s_rec = sem("denominators_ready"); s_gt = sem("gated_ready"); s_dg = sem("diag_ready"); s_bc = sem("broadcast_product"); s_gB = sem("gates_broadcast"); s_xb = sem("x_plus_bias")
        s_op = sem("o_product"); s_x1 = sem("x1_ready"); s_sq2 = sem("squares2_done"); s_rstd2 = sem("rstd2_ready"); s_xn2 = sem("xn2_ready")
        s_xnd = [sem(f"xn_stored{b}") for b in range(2)]; s_x2 = sem("xn2_transposed"); s_h2a = sem("h2T_by_act"); s_h2v = sem("h2T_by_dve")
        s_lg = sem("logits_product"); s_mask = sem("mask_ready"); s_rank = sem("rank_product")
        s_dest = sem("places_ready"); s_sct = sem("ids_scattered"); s_zero = sem("list_zeroed")
        s_cnt = sem("counts_product"); s_meta = sem("items_ready"); s_itd = sem("items_stored"); s_row = sem("items_row_loaded")
        s_brow = sem("moe_biases_loaded"); s_bt = sem("moe_biases_transposed"); s_bT = sem("biasT_ready")
        s_late = sem("late_small_loaded")
        s_lv = sem("gate_logits"); s_ge = sem("gate_exps")
        s_wl = [sem(f"piece_loaded{p}") for p in range(NPIECE)]
        s_idx = sem("ids_loaded"); s_g = sem("rows_gathered"); s_xtp = sem("rows_transposed"); s_xT = sem("xT_ready")
        s_mm = sem("step_product"); s_je = sem("up_evacuated"); s_gr = sem("glu_ready"); s_sg = sem("sigmoid_ready")
        s_act = sem("act_ready"); s_me = sem("down_evacuated"); s_ytp = sem("y_transposed"); s_ye = sem("y_evacuated")
        s_yst = sem("y_stored"); s_go = sem("gather_goes"); s_pego = sem("second_block_goes"); s_clear = sem("y_buffer_cleared")
        s_yd = sem("y_places_ready"); s_yg = [sem(f"y_gathered{b}") for b in range(NYG)]
        s_acc = sem("rows_added"); s_sq3 = sem("squares3_done"); s_rstd3 = sem("rstd3_ready"); s_ob = sem("out_ready"); s_st = [sem(f"out_stored{b}") for b in range(2)]

        groups = [("k", m, h) for m in range(2) for h in range(2)] + [("v", t, 0) for t in range(TT)] \
            + [("q", m, 0) for m in range(KT)]
        by_act = [n for n, g in enumerate(groups) if g[0] != "v"]
        by_dve = [n for n, g in enumerate(groups) if g[0] == "v"]
        mod_after = {1: (4,), 2: (5,), 3: (6,), 5: (7,), 7: (8,), 10: (9,), 12: (10,), 13: (11,)}

        def wait_group_evacuated(eng, n):
            if groups[n][0] == "v":
                eng.wait_ge(s_qv, by_dve.index(n) + 1)
            else:
                eng.wait_ge(s_qa, by_act.index(n) + 1)

        def o_start(t):
            return max(2 * KT + 2 * t, 4 * (t + 1) + 1)

        q_late = {n: (n // 2, n % 2) for n in range(2 * KT)}
        o_half = {o_start(t) + h: (t, h) for t in range(TT) for h in range(2)}
        normed = {o_start(t) + 3: t for t in range(TT)}
        x2_half = {o_start(t) + 4 + h: (t, h) for t in range(TT) for h in range(2)}
        logit_at = {o_start(t) + 6: t for t in range(TT)}
        choose_at = {o_start(t) + 7: t for t in range(TT)}
        rank_at = {o_start(t) + 7: t for t in range(TT)}
        place_at = {o_start(t) + 8: t for t in range(TT)}
        STEPS = o_start(TT - 1) + 10

        def head_at(place):
            return 2 * (place % 2) + place // 2

        w_in_v = moe_w_in.rearrange("e (k p) (s q n) -> e q p k s n", p=P, s=2, n=256)
        w_out_v = moe_w_out.rearrange("e (k p) (q n) -> e q p k n", p=P, n=512)

        def load_pieces_of(eng, e, p):
            if p < 4:
                dst = piece(p).rearrange("p (k s n) -> p k s n", k=KT, s=2)
                for s in range(2):
                    last = eng.dma_start(dst[:, :, s, :], w_in_v[e, p, :, :, s, :] if isinstance(e, int)
                                         else w_in_v[bass.ds(e, 1), p, :, :, s, :].rearrange("o p k n -> (o p) k n"))
                    last.then_inc(s_wl[p], 16)
            else:
                dst = piece(p).rearrange("p (k n) -> p k n", k=KT)
                src = w_out_v[e, p - 4] if isinstance(e, int) else \
                    w_out_v[bass.ds(e, 1), p - 4].rearrange("o p k n -> (o p) k n")
                eng.dma_start(dst, src).then_inc(s_wl[p], 16)

        def y_parts(wide):
            return [(1, 0, 1), (1, 1, 1), (0, 0, 1), (0, 1, 1)] if wide else [(0, 0, 3), (0, 1, 1)]

        steps_to = [2, 4, 6, 8, 12, 16]

        block = ctx.enter_context(nc.Block())

        @block.sync
        def _(sp):
            sp.dma_start(cT[:, :], c.rearrange("o (p t) -> p (o t)", p=P)).then_inc(s_c, 16)
            sp.dma_start(vecr[:, :], vecs).then_inc(s_vec, 16)
            mod_v = w_mod.rearrange("(p t) (q n) -> q p t n", p=P, n=MCOLS)

            def load_mod(n):
                earlier = [m for m in range(n) if stage_of[m] == stage_of[n]]
                if earlier:
                    sp.wait_ge(s_msum, earlier[-1] + 1)
                sp.dma_start(stages[stage_of[n]].rearrange("p (t n) -> p t n", t=KT), mod_v[n])\
                    .then_inc(s_mod[stage_of[n]], 16)

            def load_x(t):
                sp.dma_start(xr[:, t, :], x[t * P:(t + 1) * P, :]).then_inc(s_x[t], 16)

            load_mod(0)
            load_x(0)
            load_mod(1)
            load_x(1)
            load_mod(2)
            load_mod(3)
            for t in range(2, TT):
                load_x(t)
            wq_v = w_qkv.rearrange("(k p) n -> p k n", p=P)
            sp.dma_start(wkv, wq_v[:, :, D:QKV]).then_inc(s_wkv, 16)
            for n in range(4, 9):
                load_mod(n)
            sp.wait_ge(s_xt, 2 * TT)
            for z in range(2):
                sp.dma_start(wq[:, :, z * 512:z * 512 + 512], wq_v[:, :, z * 512:z * 512 + 512]).then_inc(s_wq, 16)
            load_mod(9)
            sp.wait_ge(s_Rs, 1)
            sp.dma_start(bias_rows_d, rowsR.rearrange("h (o n) -> h o n", o=1).to_broadcast([NQ, P, RROW])).then_inc(s_Rd, 16)
            sp.wait_ge(s_qa, 4)
            for g in range(NKV):
                here = slice(64 * (g % 2), 64 * (g % 2) + 64)
                there = slice(64 - 64 * (g % 2), 128 - 64 * (g % 2))
                sp.dma_start(kT[there, g, :], kT[here, g, :]).then_inc(s_kd, 16)
            load_mod(10)
            load_mod(11)
            sp.wait_ge(s_Rd, 16)
            sp.wait_ge(s_zero, 16)
            sp.wait_ge(s_modmm, NMOD)
            for h in range(NQ):
                g, r = h // GRP, h % GRP
                place = g * GRP + (r % 2) * 2 + r // 2
                src = bass.AP(tensor=bias_rows_d.tensor, offset=h * P * RROW + P - 1, ap=[[RROW - 1, P], [1, 2 * P]])
                sp.dma_start(relT[:, place, :], src).then_inc(s_T, 16)
            wo_v = w_o.rearrange("(k p) n -> p k n", p=P)
            for z in range(2):
                sp.wait_ge(s_qkv, len(groups) + (z + 1) * KT)
                sp.dma_start(wo[:, :, z * 512:z * 512 + 512], wo_v[:, :, z * 512:z * 512 + 512]).then_inc(s_wo[z], 16)

            def store_normed(t):
                sp.wait_ge(s_xn2, t + 1)
                sp.dma_start(xn_d[t * P:(t + 1) * P, :], xn2[:, t % 2, :]).then_inc(s_xnd[t % 2], 16)

            for t in range(TT - 2):
                store_normed(t)
            sp.wait_ge(s_pv, UNITS)
            sp.wait_ge(s_sadd, UNITS)
            sp.dma_start(brow[:, :, :], moe_b.rearrange("(r p) n -> p r n", p=P)).then_inc(s_brow, 16)
            sp.dma_start(fgB, final_g.partition_broadcast(P)).then_inc(s_late, 16)
            store_normed(TT - 2)
            store_normed(TT - 1)
            sp.wait_ge(s_op, 2 * TT)
            for p in (0, 1, 3):
                load_pieces_of(sp, 0, p)
            sp.wait_ge(s_meta, 1)
            sp.dma_start(items_d, metai[0:NITEM + 1, :]).then_inc(s_itd, 16)
            sp.wait_ge(s_itd, 16)
            sp.dma_start(items, items_d.rearrange("(o i) n -> o (i n)", o=1)).then_inc(s_row, 16)
            sp.wait_ge(s_g, 32)
            load_pieces_of(sp, 0, 2)
            load_pieces_of(sp, 0, 4)
            sp.wait_ge(s_yd, 1)
            load_pieces_of(sp, 0, 5)
            sp.wait_ge(s_row, 16)
            n_items = sp.value_load(nrow, min_val=1, max_val=NITEM)
            with sp.Fori(1, NITEM) as i:
                with sp.If(i < n_items):
                    e = sp.value_load(items[:, bass.ds(i * FIELDS, 1)], min_val=0, max_val=E - 1)
                    for p in range(NPIECE):
                        sp.wait_ge(s_mm, (i - 1) * 16 + steps_to[p])
                        load_pieces_of(sp, e, p)
            for t in range(TT):
                sp.wait_ge(s_ob, t + 1)
                sp.dma_start(out[t * P:(t + 1) * P, :], outb[:, t % 2, :]).then_inc(s_st[t % 2], 16)
            sp.wait_ge(s_st[0], TT // 2 * 16)
            sp.wait_ge(s_st[1], TT // 2 * 16)

        @block.gpsimd
        def _(pool):
            pc = [0]

            def link(ins):
                pc[0] += 1
                ins.then_inc(s_p, 1)
                pool.wait_ge(s_p, pc[0])

            pool.memset(mhalf[:, :], -0.5)
            pool.memset(ones[:, :], 1.0)
            pool.memset(ident[:, :], 0.0)
            link(pool.memset(zeros, 0))
            pool.dma_start(list_d.rearrange("(p n) o -> p (n o)", p=P), zeros).then_inc(s_zero, 16)
            pool.affine_select(out=ident[:, :], in_=ident[:, :], compare_op=ALU.not_equal, fill=1.0,
                               base=0, pattern=[[-1, P]], channel_multiplier=1)
            pool.affine_select(out=tri[:, :], in_=ones[:, :], compare_op=ALU.is_gt, fill=0.0,
                               base=0, pattern=[[1, P]], channel_multiplier=-1)
            pool.iota(tok_i[:, :], pattern=[[P, TT]], base=0, channel_multiplier=1)
            pool.iota(e_i[:, :], pattern=[[1, E]], base=0, channel_multiplier=0)
            pool.iota(p_i[:, :], pattern=[[0, 1]], base=0, channel_multiplier=1).then_inc(s_const, 1)
            def rstd_of(first, n):
                link(pool.tensor_scalar(var[:, first:first + n], ss[:, first:first + n], 1.0 / D, EPS, ALU.mult, ALU.add))
                return pool.tensor_tensor(out=rstd[:, first:first + n], in0=var[:, first:first + n],
                                          in1=mhalf[:, 0:n], op=ALU.pow)

            for t in range(TT):
                pool.wait_ge(s_sq, t + 1)
                rstd_of(t, 1).then_inc(s_rstd, 1)
            pool.wait_ge(s_gB, 1)
            for t in range(TT):
                pool.tensor_tensor(out=xr[:, t, :], in0=xr[:, t, :], in1=gboB, op=ALU.add).then_inc(s_xb, 1)
            pool.wait_ge(s_zero, 16)
            for n in range(TT + 3):
                if n < TT:
                    pool.wait_ge(s_sq2, n + 1)
                    rstd_of(TT + n, 1).then_inc(s_rstd2, 1)
                t = n - 3
                if t < 0:
                    continue
                pool.wait_ge(s_dest, t + 1)
                for j in range(TOPK):
                    n = t * TOPK + j
                    pool.indirect_dma_start(out=list_d, out_offset=bass.IndirectOffsetOnAxis(ap=dest[:, n:n + 1], axis=0),
                                            in_=tok_i[:, t:t + 1].bitcast(u32), in_offset=None).then_inc(s_sct, 16)
            pool.wait_ge(s_sct, TT * TOPK * 16)
            for b in range(2):
                pool.wait_ge(s_xnd[b], TT // 2 * 16)

            def load_ids(start):
                with nc.allow_non_contiguous_dma(reason="one id per partition"):
                    src = list_d[bass.ds(start, ITEM), :].rearrange("(b p) o -> p (b o)", p=P)
                    pool.dma_start(idx, src).then_inc(s_idx, 16)

            def gather_rows():
                for b in range(2):
                    pool.indirect_dma_start(out=xg[:, b, :], out_offset=None, in_=xn_d,
                                            in_offset=bass.IndirectOffsetOnAxis(ap=idx[:, b:b + 1], axis=0))\
                        .then_inc(s_g, 16)

            load_ids(0)
            pool.wait_ge(s_idx, 16)
            gather_rows()
            pool.wait_ge(s_pv, UNITS)
            pool.memset(ysb[:, :, :], 0.0).then_inc(s_clear, 1)
            pool.wait_ge(s_clear, 1)
            pool.dma_start(y_d[0:1, 0:P], ysb[0:1, 0, 0:P]).then_inc(s_yst, 16)
            pool.wait_ge(s_row, 16)
            n_items = pool.value_load(nrow, min_val=1, max_val=NITEM)
            with pool.Fori(0, NITEM) as i:
                with pool.If(i < n_items):
                    start = pool.value_load(items[:, bass.ds(i * FIELDS + FIELDS + 1, 1)], min_val=0, max_val=E * SEQ - ITEM)
                    width = pool.value_load(items[:, bass.ds(i * FIELDS + 2, 1)], min_val=0, max_val=len(WIDTHS) - 1)
                    pool.wait_ge(s_g, (i + 1) * 32)
                    load_ids(start)
                    pool.wait_ge(s_idx, (i + 2) * 16)
                    pool.wait_ge(s_xtp, (i + 1) * 4)
                    pool.sem_inc(s_go, 1)
                    gather_rows()
                    first = pool.value_load(items[:, bass.ds(i * FIELDS + 4, 1)], min_val=0, max_val=SEQ * TOPK)
                    row = y_d[bass.ds(first, ITEM), :].rearrange("(b p) n -> p b n", p=P)
                    with pool.If(width < NARROW):
                        pool.wait_ge(s_ye, i * 5 + 9)
                        pool.dma_start(row[:, 0, :], ysb[:, 0, :]).then_inc(s_yst, 16)
                    with pool.If(width >= NARROW):
                        pool.wait_ge(s_ye, i * 5 + 9)
                        pool.dma_start(row, ysb[:, :, :]).then_inc(s_yst, 16)
            pool.wait_ge(s_yst, (n_items + 1) * 16)
            pool.sem_inc(s_go, 1)
            pool.wait_ge(s_yd, 1)

            def gather_outputs(t):
                if t >= NYG:
                    pool.wait_ge(s_acc, t - NYG + 1)
                    pool.sem_inc(s_go, 1)
                for j in range(TOPK):
                    n = t * TOPK + j
                    pool.indirect_dma_start(out=yg[:, t % NYG, j, :], out_offset=None, in_=y_d[0:SEQ * TOPK, :],
                                            in_offset=bass.IndirectOffsetOnAxis(ap=ydest[:, n:n + 1], axis=0))\
                        .then_inc(s_yg[t % NYG], 16)

            for t in range(NYG - 1):
                gather_outputs(t)
            for t in range(TT):
                if t + NYG - 1 < TT:
                    gather_outputs(t + NYG - 1)
                pool.wait_ge(s_sq3, t + 1)
                rstd_of(2 * TT + t, 1).then_inc(s_rstd3, 1)

        @block.scalar
        def _(act):
            ac = [0]

            def link(ins):
                ac[0] += 1
                ins.then_inc(s_a, 1)
                act.wait_ge(s_a, ac[0])

            act.dma_start(table[:, :], rel_table).then_inc(s_small, 16)
            act.dma_start(bucketR, bucket_rows).then_inc(s_small, 16)
            act.dma_start(fillR, window_fill).then_inc(s_small, 16)
            act.dma_start(sinkB[:, :], sinks.partition_broadcast(P)).then_inc(s_small, 16)
            act.dma_start(bvB[:, :], vecs.rearrange("r n -> (r n)")[(V_BQKV + 10) * P:(V_BQKV + 12) * P]
                           .partition_broadcast(P)).then_inc(s_small, 16)
            act.dma_start(brB[:, :], router_b.partition_broadcast(P)).then_inc(s_small, 16)
            act.dma_start(wr[:, :, :], router_w.rearrange("(k p) n -> p k n", p=P)).then_inc(s_small, 16)
            act.wait_ge(s_c, 16)
            act.activation(cS[:, :], cT[:, :], ACT.Sigmoid).then_inc(s_cs, 1)
            act.wait_ge(s_vT, 1)
            act.activation(vecT[:, :], bank(6)[:, 0:V_N], ACT.Copy).then_inc(s_vecT, 1)
            for t in range(TT + 1):
                if t < TT:
                    act.wait_ge(s_x[t], 16)
                    if t:
                        act.wait_ge(s_sq, t)
                    act.activation(junk1, xr[:, t, :], ACT.Square, accum_out=ss[:, t:t + 1]).then_inc(s_sq, 1)
                if t >= 1:
                    act.wait_ge(s_rstd, t)
                    act.activation(xn1[:, t - 1, :], xr[:, t - 1, :], ACT.Copy, scale=rstd[:, t - 1:t]).then_inc(s_xn, 1)
            act.wait_ge(s_coef, 1)
            for t in range(TT):
                act.wait_ge(s_xt, 2 * t + 1)
                for k in range(4):
                    last = act.activation(hT[:, k, t * P:(t + 1) * P], bank(2 * t % 4)[:, k * P:(k + 1) * P],
                                          ACT.Identity, scale=Am[:, k:k + 1], bias=modT[:, k:k + 1])
                last.then_inc(s_hta, 1)
            for n in by_act:
                kind, m, h = groups[n]
                act.wait_ge(s_qkv, n + 1)
                if kind == "k":
                    for z in range(2):
                        part = slice(64 * z, 64 * z + 64)
                        last = act.activation(kT[part, 2 * m + z, h * 512:h * 512 + 512], bank(n % 4)[part, :], ACT.Identity,
                                              bias=vecT[part, V_BQKV + 8 + m:V_BQKV + 9 + m])
                else:
                    if m == 0:
                        act.wait_ge(s_msum, NMOD)
                    last = act.activation(qT[:, 0, m, :], bank(n % 4), ACT.Identity, scale=0.125, bias=bq8[:, m:m + 1])
                last.then_inc(s_qa, 1)

            def probs_evacuate(u):
                act.wait_ge(s_ptr, u + 1)
                if u >= 2:
                    act.wait_ge(s_pv, u - 1)
                src = bank(4).rearrange("p (h k n) -> p h k n", h=2, k=2)
                dst = probsT[:, u % 2, 0:512].rearrange("p (h k n) -> p h k n", h=2, k=2)
                lo_k = 0 if u // NKV else 1
                act.activation(dst[:, :, lo_k:, :], src[:, :, lo_k:, :], ACT.Copy).then_inc(s_pta, 1)

            def heads_evacuate(u):
                b, g = u // NKV, u % NKV
                act.wait_ge(s_ot, u + 1)
                act.activation(attnT[:, 2 * g:2 * g + 2, b * P:(b + 1) * P],
                               bank(6)[:, 0:256].rearrange("p (m n) -> p m n", m=2), ACT.Copy).then_inc(s_at, 1)

            def exps(u):
                z = 0 if u // NKV else P
                act.wait_ge(s_nm, u + 1)
                for r in range(GRP):
                    act.activation(scores[:, u % 2, r, z:], scores[:, u % 2, r, z:], ACT.Exp,
                                   bias=negm[:, u % 2, r:r + 1], accum_out=rs[:, u % 2, r:r + 1])
                act.activation(es[:, u % 2, :], dsk[:, u % 2, :], ACT.Exp).then_inc(s_exp, 1)

            def squares2(t):
                act.wait_ge(s_x1, 2 * t + 2)
                if t:
                    act.wait_ge(s_sq2, t)
                act.activation(junk2, xr[:, t, :], ACT.Square, accum_out=ss[:, TT + t:TT + t + 1]).then_inc(s_sq2, 1)

            def h2_evacuate(t, h):
                act.wait_ge(s_x2, 2 * t + h + 1)
                if t >= 2 and h == 0:
                    act.wait_ge(s_lg, t - 1)
                for k in range(4 * h, 4 * h + 4):
                    last = act.activation(h2T[:, t % 2, k, :], bank(2)[:, (k % 4) * P:(k % 4 + 1) * P], ACT.Identity,
                                          scale=Af[:, k:k + 1], bias=modT[:, 24 + k:25 + k])
                last.then_inc(s_h2a, 1)

            exps(0)
            for u in range(STEPS):
                if 1 <= u <= UNITS:
                    probs_evacuate(u - 1)
                if 2 <= u <= UNITS + 1:
                    heads_evacuate(u - 2)
                if u + 1 < UNITS:
                    exps(u + 1)
                if u - 1 in q_late:
                    m, z = q_late[u - 1]
                    act.wait_ge(s_qkv, len(groups) + u)
                    act.activation(qT[:, 1, m, z * 256:z * 256 + 256], bank(7)[:, 0:256], ACT.Identity, scale=0.125,
                                   bias=bq8[:, m:m + 1])\
                        .then_inc(s_qa, 1)
                if u in normed:
                    squares2(normed[u])
                if u - 1 in x2_half:
                    h2_evacuate(*x2_half[u - 1])
            act.wait_ge(s_lv, 1)
            act.activation(gates[:, :, :], gates[:, :, :], ACT.Exp).then_inc(s_ge, 1)

            def rows_evacuate(n, ks, done):
                for k in ks:
                    if k % 2 == 0:
                        act.wait_ge(s_xtp, done + (k - ks[0]) // 2 + 1)
                    act.activation(xT[:, k, 0:n], bank(4 + k // 2 % 2)[:, (k % 2) * 256:(k % 2) * 256 + n], ACT.Identity,
                                   scale=Af[:, k:k + 1], bias=modT[:, 24 + k:25 + k]).then_inc(s_xT, 1)

            act.wait_ge(s_lg, TT)
            act.activation(yT[:, 7, 0:P], ident[:, :], ACT.Copy)
            act.activation(yT[:, 7, P:], ident[:, :], ACT.Copy).then_inc(s_me, 8)
            rows_evacuate(ITEM, range(4), 0)
            act.wait_ge(s_row, 16)
            n_items = act.value_load(nrow, min_val=1, max_val=NITEM)

            def item(i, n):
                rows_evacuate(n, range(4, 8), i * 4 + 2)
                for j in range(8):
                    act.wait_ge(s_gr, i * 8 + j + 1)
                    act.activation(sbuf_[:, j % 2, 0:n], gbuf[:, j % 2, 0:n], ACT.Sigmoid, scale=1.702)\
                        .then_inc(s_sg, 1)

                for m in range(8):
                    act.wait_ge(s_mm, i * 16 + 8 + m + 1)
                    act.activation(yT[:, m, 0:n], bank(m % 4)[:, 0:n], ACT.Identity, scale=modT[:, 40 + m:41 + m],
                                   bias=bias_now[:, 16 + m:17 + m]).then_inc(s_me, 1)
                    if m == (4 if n > P else 7):
                        rows_evacuate(ITEM, range(4), i * 4 + 4)

            with act.Fori(0, NITEM) as i:
                with act.If(i < n_items):
                    width = act.value_load(items[:, bass.ds(i * FIELDS + 2, 1)], min_val=0, max_val=len(WIDTHS) - 1)
                    by_width(act, width, lambda w: item(i, WIDTHS[w]))
            for t in range(TT):
                act.wait_ge(s_acc, t + 1)
                if t:
                    act.wait_ge(s_sq3, t)
                act.activation(junk3, xr[:, t, :], ACT.Square, accum_out=ss[:, 16 + t:17 + t]).then_inc(s_sq3, 1)

        @block.vector
        def _(dve):
            vc = [0]

            def link(ins):
                vc[0] += 1
                ins.then_inc(s_v, 1)
                dve.wait_ge(s_v, vc[0])

            dve.wait_ge(s_cs, 1)
            dve.tensor_tensor(out=cA[:, :], in0=cT[:, :], in1=cS[:, :], op=ALU.mult).then_inc(s_ca, 1)
            dve.wait_ge(s_ca, 1)
            dve.wait_ge(s_const, 1)
            dve.tensor_copy(p_f[:, :], p_i[:, :])
            link(dve.tensor_copy(e_f[:, :], e_i[:, :]))
            dve.tensor_scalar(e1k[:, :], e_f[:, :], float(SEQ), None, ALU.mult)
            dve.wait_ge(s_vecT, 1)
            dve.tensor_scalar(bq8[:, :], vecT[:, V_BQKV:V_BQKV + 8], 0.125, None, ALU.mult)

            def mod_evacuate(n):
                dve.wait_ge(s_modmm, n + 1)
                dve.tensor_tensor(out=modT[:, 4 * n:4 * n + 4], in0=bank(6 + n % 2)[:, 4 * n:4 * n + 4],
                                  in1=vecT[:, 4 * n:4 * n + 4], op=ALU.add).then_inc(s_modT, 1)
                dve.wait_ge(s_modT, n + 1)

            def mod_sum_of(n):
                b = stage_of[n]
                dve.wait_ge(s_mod[b], 16 * (stage_of[:n].count(b) + 1))
                if n >= 2:
                    dve.wait_ge(s_modmm, n - 1)
                w = stages[b].rearrange("p (t n) -> p t n", t=KT)
                link(dve.tensor_scalar(mod_sum[:, n % 2, :], w[:, 0, :], cA[:, 0:1], None, ALU.mult))
                for t in range(1, KT):
                    ins = dve.scalar_tensor_tensor(out=mod_sum[:, n % 2, :], in0=w[:, t, :], scalar=cA[:, t:t + 1],
                                                   in1=mod_sum[:, n % 2, :], op0=ALU.mult, op1=ALU.add)
                    if t < KT - 1:
                        link(ins)
                    else:
                        ins.then_inc(s_msum, 1)

            for n in range(4):
                mod_sum_of(n)
                if n:
                    mod_evacuate(n - 1)
            mod_evacuate(3)
            link(dve.scalar_tensor_tensor(out=Am[:, :], in0=modT[:, 8:16], scalar=1.0,
                                          in1=vecT[:, V_GMIX:V_GMIX + 8], op0=ALU.add, op1=ALU.mult))
            dve.engine_nop().then_inc(s_coef, 1)

            for t in range(TT):
                dve.wait_ge(s_xt, 2 * t + 2)
                for k in range(4, 8):
                    last = dve.tensor_scalar(hT[:, k, t * P:(t + 1) * P], bank((2 * t + 1) % 4)[:, (k - 4) * P:(k - 3) * P],
                                             Am[:, k:k + 1], modT[:, k:k + 1], ALU.mult, ALU.add)
                last.then_inc(s_htv, 1)
            dve.wait_ge(s_small, 112)
            dve.tensor_scalar(nsink[:, :].rearrange("p (g a r) -> p g a r", g=NKV, a=2),
                              sinkB[:, :].rearrange("p (g r a) -> p g a r", g=NKV, a=2), -1.0, None, ALU.mult)
            dve.wait_ge(s_R, 1)
            dve.tensor_tensor(out=rowsR, in0=bank(5)[0:NQ, 0:RROW], in1=fillR, op=ALU.add).then_inc(s_Rs, 1)
            mod_sum_of(4)
            mod_sum_of(5)
            for n, (kind, t, _) in enumerate(groups):
                if kind == "v":
                    dve.wait_ge(s_qkv, n + 1)
                    dve.tensor_tensor(out=vv[:, t, :], in0=bank(n % 4)[:, 0:256], in1=bvB[:, :], op=ALU.add)\
                        .then_inc(s_qv, 1)
                for piece_n in mod_after.get(n, ()):
                    mod_evacuate(piece_n)
                    if piece_n + 2 < NMOD:
                        mod_sum_of(piece_n + 2)
            dve.scalar_tensor_tensor(out=Af[:, :], in0=modT[:, 32:40], scalar=1.0,
                                     in1=vecT[:, V_GFFN:V_GFFN + 8], op0=ALU.add, op1=ALU.mult)
            link(dve.tensor_tensor(out=gbo[:, :], in0=modT[:, 16:24], in1=vecT[:, V_BO:V_BO + 8], op=ALU.mult))

            for n in range(2 * KT):
                k = n % KT
                col = modT[:, 16 + k:17 + k] if n < KT else gbo[:, k:k + 1]
                if n >= 2:
                    dve.wait_ge(s_bc, n - 1)
                dve.tensor_scalar(diag[:, n % 2, :], ident[:, :], col, None, ALU.mult).then_inc(s_dg, 1)
            dve.wait_ge(s_bc, 2 * KT)
            dve.tensor_copy(gmB, bank(4, 2))
            dve.tensor_copy(gboB, bank(6, 2)).then_inc(s_gB, 1)
            dve.wait_ge(s_T, NQ * 16)

            def scores_in(u):
                b, g = u // NKV, u % NKV
                z = 0 if b else P
                dve.wait_ge(s_sc, u + 1)
                if u >= 2:
                    dve.wait_ge(s_ptr, u - 1)
                s = scores[:, u % 2, :, z:]
                src = bank(0, 2).rearrange("p (h n) -> p h n", h=GRP)[:, :, z:]
                dve.tensor_tensor(out=s, in0=src, in1=relT[:, g * GRP:(g + 1) * GRP, z:], op=ALU.add).then_inc(s_sadd, 1)
                dve.wait_ge(s_sadd, u + 1)
                link(dve.tensor_reduce(out=mx[:, u % 2, :], in_=s, axis=AX.X, op=ALU.max))
                link(dve.scalar_tensor_tensor(out=negm[:, u % 2, :], in0=mx[:, u % 2, :], scalar=-1.0,
                                              in1=nsink[:, g * GRP:(g + 1) * GRP], op0=ALU.mult, op1=ALU.min))
                dve.tensor_tensor(out=dsk[:, u % 2, :], in0=negm[:, u % 2, :], in1=nsink[:, g * GRP:(g + 1) * GRP],
                                  op=ALU.subtract).then_inc(s_nm, 1)

            def probs_out(u):
                lo_k = 0 if u // NKV else 1
                dve.wait_ge(s_ptr, u + 1)
                if u >= 2:
                    dve.wait_ge(s_pv, u - 1)
                src = bank(5).rearrange("p (h k n) -> p h k n", h=2, k=2)
                dst = probsT[:, u % 2, 512:1024].rearrange("p (h k n) -> p h k n", h=2, k=2)
                dve.tensor_copy(dst[:, :, lo_k:, :], src[:, :, lo_k:, :]).then_inc(s_ptv, 1)
                link(dve.tensor_tensor(out=den[:, u % 2, :], in0=rs[:, u % 2, :], in1=es[:, u % 2, :], op=ALU.add))
                dve.reciprocal(rec[:, u % 2, :], den[:, u % 2, :]).then_inc(s_rec, 1)

            def heads_out(u):
                dve.wait_ge(s_rec, u + 1)
                dve.wait_ge(s_pv, u + 1)
                if u >= 2:
                    dve.wait_ge(s_ot, u - 1)
                src = bank(6)[:, 0:256].rearrange("p (a r d) -> p a r d", a=2, r=2)
                dst = heads[:, u % 2, :].rearrange("p (r a d) -> p a r d", a=2, r=2)
                by = rec[:, u % 2, :].rearrange("p (a r o) -> p a r o", a=2, o=1).to_broadcast([P, 2, 2, HD])
                dve.tensor_tensor(out=dst, in0=src, in1=by, op=ALU.mult).then_inc(s_o, 1)

            def residual(t, h):
                cols = slice(h * 512, h * 512 + 512)
                dve.wait_ge(s_op, 2 * t + h + 1)
                dve.tensor_tensor(out=gated, in0=bank(7), in1=gmB[:, cols], op=ALU.mult).then_inc(s_gt, 1)
                dve.wait_ge(s_gt, 2 * t + h + 1)
                dve.wait_ge(s_xb, t + 1)
                dve.tensor_tensor(out=xr[:, t, cols], in0=xr[:, t, cols], in1=gated, op=ALU.add).then_inc(s_x1, 1)

            def norm2(t):
                dve.wait_ge(s_rstd2, t + 1)
                if t >= 2:
                    dve.wait_ge(s_x2, 2 * (t - 1))
                    dve.wait_ge(s_xnd[t % 2], 16 * (t // 2))
                dve.tensor_scalar(xn2[:, t % 2, :], xr[:, t, :], rstd[:, TT + t:TT + t + 1], None, ALU.mult)\
                    .then_inc(s_xn2, 1)

            def choose(t):
                dve.wait_ge(s_lg, t + 1)
                link(dve.tensor_tensor(out=lg[:, :], in0=bank(3)[:, 0:E], in1=brB[:, :], op=ALU.add))
                link(dve.max(out=top8[:, t, :], in_=lg[:, :]))
                link(dve.max_index(out=idx8[:, :], in_max=top8[:, t, :], in_values=lg[:, :]))
                link(dve.tensor_copy(idxf[:, :], idx8[:, :]))
                link(dve.tensor_tensor(out=onehot[:, t, :, :],
                                       in0=idxf[:, 0:TOPK].rearrange("p (j o) -> p j o", o=1).to_broadcast([P, TOPK, E]),
                                       in1=e_f[:, :].rearrange("p (o e) -> p o e", o=1).to_broadcast([P, TOPK, E]),
                                       op=ALU.is_equal))
                dve.tensor_reduce(out=mask[:, t, :], in_=onehot[:, t, :, :].rearrange("p j e -> p e j"), axis=AX.X,
                                  op=ALU.add).then_inc(s_mask, 1)
                dve.wait_ge(s_mask, t + 1)
                if t:
                    link(dve.tensor_tensor(out=macc[:, t, :], in0=macc[:, t - 1, :], in1=mask[:, t, :], op=ALU.add))
                else:
                    link(dve.tensor_copy(macc[:, 0, :], mask[:, 0, :]))

            def places(t):
                dve.wait_ge(s_rank, t + 1)
                link(dve.tensor_tensor(out=pos[:, :], in0=bank(3)[:, 0:E], in1=e1k[:, :], op=ALU.add))
                link(dve.tensor_tensor(out=ohp[:, :, :], in0=onehot[:, t, :, :],
                                       in1=pos[:, :].rearrange("p (o e) -> p o e", o=1).to_broadcast([P, TOPK, E]),
                                       op=ALU.mult))
                link(dve.tensor_reduce(out=destf[:, t * TOPK:(t + 1) * TOPK], in_=ohp[:, :, :], axis=AX.X, op=ALU.add))
                dve.tensor_copy(dest[:, t * TOPK:(t + 1) * TOPK], destf[:, t * TOPK:(t + 1) * TOPK]).then_inc(s_dest, 1)

            scores_in(0)
            for u in range(STEPS):
                if 1 <= u <= UNITS:
                    probs_out(u - 1)
                if u + 1 < UNITS:
                    scores_in(u + 1)
                if u in place_at:
                    places(place_at[u])
                if u - 1 in o_half:
                    residual(*o_half[u - 1])
                if 1 <= u <= UNITS:
                    heads_out(u - 1)
                if u in normed:
                    norm2(normed[u])
                if u in choose_at:
                    choose(choose_at[u])

            dve.wait_ge(s_cnt, 1)
            nb, cnt = lo[:, 0, :], lo[:, 1, :]
            link(dve.tensor_copy(cnt, bank(3)[:, 64:64 + E]))
            link(dve.tensor_scalar(nb, cnt, 0.0, None, ALU.is_gt))
            for over in range(ITEM, SEQ, ITEM):
                link(dve.scalar_tensor_tensor(out=nb, in0=cnt, scalar=float(over), in1=nb, op0=ALU.is_gt, op1=ALU.add))
            link(dve.tensor_scalar(nb[:, 0:1], nb[:, 0:1], 1.0, None, ALU.max))
            link(dve.tensor_copy(lo[:, 2:4, :], lo[:, 0:2, :]))
            cur = 2
            for step in (1, 2, 4, 8, 16):
                nxt = 6 - cur
                dve.tensor_copy(lo[:, nxt:nxt + 2, 0:step], lo[:, cur:cur + 2, 0:step])
                link(dve.tensor_tensor(out=lo[:, nxt:nxt + 2, step:], in0=lo[:, cur:cur + 2, step:],
                                       in1=lo[:, cur:cur + 2, 0:E - step], op=ALU.add))
                cur = nxt
            ends = lo[:, cur, :]
            starts, ystarts = lo[:, 6, :], lo[:, 7, :]
            link(dve.tensor_tensor(out=lo[:, 6:8, :], in0=lo[:, cur:cur + 2, :], in1=lo[:, 0:2, :], op=ALU.subtract))
            le, rel, mine, junk = lo[:, 8, :], lo[:, 9, :], lo[:, 10, :], lo[:, 11, :]
            dve.tensor_scalar(le, starts, p_f[:, 0:1], None, ALU.is_le)
            link(dve.tensor_scalar(rel, starts, -1.0, p_f[:, 0:1], ALU.mult, ALU.add))
            link(dve.scalar_tensor_tensor(out=mine, in0=ends, scalar=p_f[:, 0:1], in1=le, op0=ALU.is_gt, op1=ALU.mult))
            dve.scalar_tensor_tensor(out=lo[:, 12, :], in0=rel, scalar=float(ITEM), in1=e1k[:, :], op0=ALU.mult, op1=ALU.add)
            dve.scalar_tensor_tensor(out=lo[:, 13, :], in0=rel, scalar=float(ITEM), in1=ystarts, op0=ALU.mult, op1=ALU.add)
            link(dve.scalar_tensor_tensor(out=lo[:, 14, :], in0=rel, scalar=-float(ITEM), in1=cnt, op0=ALU.mult, op1=ALU.add))
            for col, src in ((0, e_f[:, :]), (1, lo[:, 12, :]), (4, lo[:, 13, :]), (2, lo[:, 14, :])):
                link(dve.scalar_tensor_tensor(out=junk, in0=mine, scalar=1.0, in1=src, op0=ALU.mult, op1=ALU.mult,
                                              accum_out=meta[:, col:col + 1]))
            link(dve.tensor_copy(junk[:, 0:1], meta[:, 2:3]))
            link(dve.tensor_scalar(meta[:, 2:3], junk[:, 0:1], float(WIDTHS[0]), None, ALU.is_gt))
            for w in WIDTHS[1:-1]:
                link(dve.scalar_tensor_tensor(out=meta[:, 2:3], in0=junk[:, 0:1], scalar=float(w), in1=meta[:, 2:3],
                                              op0=ALU.is_gt, op1=ALU.add))
            link(dve.tensor_copy(meta[:, 3:4], ends[:, E - 1:E]))
            dve.tensor_copy(metai, meta).then_inc(s_meta, 1)
            val = lo[:, 15, :]
            link(dve.tensor_tensor(out=val, in0=ystarts, in1=e1k[:, :], op=ALU.subtract))
            link(dve.tensor_tensor(out=ohpos[:, :, :, :].rearrange("p t j e -> p (t j) e"),
                                   in0=onehot[:, :, :, :].rearrange("p t j e -> p (t j) e"),
                                   in1=val.rearrange("p (o e) -> p o e", o=1).to_broadcast([P, TT * TOPK, E]), op=ALU.mult))
            link(dve.tensor_reduce(out=ydf, in_=ohpos[:, :, :, :].rearrange("p t j e -> p (t j) e"), axis=AX.X, op=ALU.add))
            link(dve.tensor_tensor(out=ydf, in0=ydf, in1=destf[:, :], op=ALU.add))
            dve.tensor_copy(ydest, ydf).then_inc(s_yd, 1)
            link(dve.tensor_tensor(out=gates[:, :, :], in0=top8[:, :, 0:TOPK],
                                   in1=top8[:, :, 0:1].to_broadcast([P, TT, TOPK]), op=ALU.subtract))
            dve.engine_nop().then_inc(s_lv, 1)
            dve.wait_ge(s_bt, 1)
            bsrc = bank(0, 2)[:, 0:768].rearrange("p (e n) -> p e n", e=E)
            dve.tensor_copy(biasT[:, :, 0:8], bsrc[:, :, 0:8])
            dve.tensor_scalar(biasT[:, :, 8:16], bsrc[:, :, 8:16], 1.0, None, ALU.add)
            link(dve.tensor_tensor(out=biasT[:, :, 16:24], in0=bsrc[:, :, 16:24],
                                   in1=modT[:, 40:48].rearrange("p (o n) -> p o n", o=1).to_broadcast([P, E, 8]), op=ALU.mult))
            dve.engine_nop().then_inc(s_bT, 1)
            dve.wait_ge(s_ge, 1)
            link(dve.tensor_reduce(out=gsum, in_=gates[:, :, :], axis=AX.X, op=ALU.add))
            link(dve.reciprocal(gsum, gsum))
            link(dve.tensor_tensor(out=gates[:, :, :], in0=gates[:, :, :],
                                   in1=gsum.rearrange("p (t o) -> p t o", o=1).to_broadcast([P, TT, TOPK]), op=ALU.mult))

            dve.wait_ge(s_clear, 1)
            dve.engine_nop().then_inc(s_ye, 3)
            dve.wait_ge(s_row, 16)
            n_items = dve.value_load(nrow, min_val=1, max_val=NITEM)
            before = vc[0]

            def last_tile_out(i):
                dve.wait_ge(s_ytp, i * 5 + 1)
                dve.tensor_copy(ysb[:, 1, 7 * P:], bank(7)[:, 0:P])
                dve.tensor_copy(ysb[:, 0, 7 * P:], bank(7)[:, 3 * P:4 * P]).then_inc(s_ye, 1)

            def item(i, e, n, wide):
                k = [0]
                per_item = 1 + 8

                def link_i(ins):
                    k[0] += 1
                    ins.then_inc(s_v, 1)
                    dve.wait_ge(s_v, i * per_item + (before + k[0]))

                last_tile_out(i)
                link_i(dve.tensor_copy(bias_now, biasT[:, bass.ds(e, 1), :].rearrange("p o n -> p (o n)")))

                def up(j):
                    dve.wait_ge(s_mm, i * 16 + j + 1)
                    dve.tensor_scalar(gbuf[:, j % 2, 0:n], bank(j % 4)[:, 0:n], bias_now[:, j:j + 1], 7.0,
                                      ALU.add, ALU.min).then_inc(s_gr, 1)
                    dve.tensor_scalar(lbuf[j % 3][:, 0:n], bank(j % 4)[:, 256:256 + n], bias_now[:, 8 + j:9 + j], -6.0,
                                      ALU.add, ALU.max).then_inc(s_je, 1)

                def activate(j):
                    dve.wait_ge(s_sg, i * 8 + j + 1)
                    link_i(dve.tensor_tensor(out=gsbuf[:, j % 2, 0:n], in0=gbuf[:, j % 2, 0:n],
                                             in1=sbuf_[:, j % 2, 0:n], op=ALU.mult))
                    dve.scalar_tensor_tensor(out=actT[:, j, 0:n], in0=lbuf[j % 3][:, 0:n], scalar=8.0,
                                             in1=gsbuf[:, j % 2, 0:n], op0=ALU.min, op1=ALU.mult).then_inc(s_act, 1)

                for j in range(9):
                    if j < 8:
                        up(j)
                    if j >= 1:
                        activate(j - 1)
                dve.wait_ge(s_yst, i * 16 + 16)
                so_far = 1
                for b, h, done in y_parts(wide):
                    rows = n - P if b else P
                    cols = 512 - h * P
                    so_far += done
                    dve.wait_ge(s_ytp, i * 5 + so_far)
                    dve.tensor_copy(ysb[0:rows, b, h * 512:h * 512 + cols], bank((4 if b else 6) + h)[0:rows, 0:cols])\
                        .then_inc(s_ye, done)

            with dve.Fori(0, NITEM) as i:
                with dve.If(i < n_items):
                    e = dve.value_load(items[:, bass.ds(i * FIELDS, 1)], min_val=0, max_val=E - 1)
                    width = dve.value_load(items[:, bass.ds(i * FIELDS + 2, 1)], min_val=0, max_val=len(WIDTHS) - 1)
                    by_width(dve, width, lambda w: item(i, e, WIDTHS[w], w >= NARROW))
                    with dve.If(i >= n_items - 1):
                        last_tile_out(i + 1)

            dve.wait_ge(s_late, 16)
            s_done = s_dg
            dc = [2 * KT]

            def link_last(ins):
                dc[0] += 1
                ins.then_inc(s_done, 1)
                dve.wait_ge(s_done, dc[0])

            def finish(t):
                dve.wait_ge(s_rstd3, t + 1)
                if t >= 2:
                    dve.wait_ge(s_st[t % 2], 16 * (t // 2))
                dve.scalar_tensor_tensor(out=outb[:, t % 2, :], in0=xr[:, t, :], scalar=rstd[:, 16 + t:17 + t],
                                         in1=fgB, op0=ALU.mult, op1=ALU.mult).then_inc(s_ob, 1)

            for t in range(TT + 1):
                if t < TT:
                    dve.wait_ge(s_yg[t % NYG], 64 * (t // NYG + 1))
                    for j in range(TOPK):
                        ins = dve.scalar_tensor_tensor(out=xr[:, t, :], in0=yg[:, t % NYG, j, :], scalar=gates[:, t, j:j + 1],
                                                       in1=xr[:, t, :], op0=ALU.mult, op1=ALU.add)
                        if j < TOPK - 1:
                            link_last(ins)
                        else:
                            ins.then_inc(s_acc, 1)
                if t >= 1:
                    finish(t - 1)

        @block.tensor
        def _(pe):
            pe.wait_ge(s_const, 1)
            pe.wait_ge(s_vec, 16)
            pe.transpose(bank(6)[:, 0:V_N], vecr[:, :], ident[0:V_N, 0:V_N]).then_inc(s_vT, 1)

            def mod_products(n):
                if n == 0:
                    pe.wait_ge(s_vecT, 1)
                elif n >= 2:
                    pe.wait_ge(s_modT, n - 1)
                pe.wait_ge(s_msum, n + 1)
                for q in range(4):
                    last = pe.matmul(bank(6 + n % 2)[:, 4 * n + q:4 * n + q + 1],
                                     mod_sum[:, n % 2, q * P:(q + 1) * P], ones[:, 0:1], start=True, stop=True)
                last.then_inc(s_modmm, 1)

            for n in range(4):
                mod_products(n)
            pe.wait_ge(s_small, 112)
            pe.matmul(bank(5)[0:NQ, 0:RROW], table[:, :], bucketR, start=True, stop=True).then_inc(s_R, 1)
            for t in range(TT):
                pe.wait_ge(s_xn, t + 1)
                for h in range(2):
                    n = 2 * t + h
                    if n >= 4:
                        pe.wait_ge(s_htv if h else s_hta, (n - 4) // 2 + 1)
                    for k in range(4):
                        last = pe.transpose(bank(n % 4)[:, k * P:(k + 1) * P],
                                            xn1[:, t, (4 * h + k) * P:(4 * h + k + 1) * P], ident[:, :])
                    last.then_inc(s_xt, 1)
            pe.wait_ge(s_wkv, 16)
            pe.wait_ge(s_hta, TT)
            pe.wait_ge(s_htv, TT)
            for n, (kind, m, h) in enumerate(groups):
                if n >= 4:
                    wait_group_evacuated(pe, n - 4)
                if n == by_dve[-1] + 1:
                    pe.wait_ge(s_wq, 32)
                for k in range(KT):
                    if kind == "v":
                        last = pe.matmul(bank(n % 4)[:, 0:256], hT[:, k, m * P:(m + 1) * P], wkv[:, k, 256:512],
                                         start=(k == 0), stop=(k == KT - 1))
                    else:
                        w = wq if kind == "q" else wkv
                        last = pe.matmul(bank(n % 4), w[:, k, m * P:(m + 1) * P], hT[:, k, h * 512:h * 512 + 512],
                                         start=(k == 0), stop=(k == KT - 1))
                last.then_inc(s_qkv, 1)
                for piece_n in mod_after.get(n, ()):
                    mod_products(piece_n)
            pe.wait_ge(s_modT, NMOD)
            for n in range(2 * KT):
                pe.wait_ge(s_dg, n + 1)
                pe.matmul(bank(4, 4)[:, n * P:(n + 1) * P], ones[:, :], diag[:, n % 2, :], start=True, stop=True)\
                    .then_inc(s_bc, 1)

            def scores_product(u):
                b, g = u // NKV, u % NKV
                if u >= 1:
                    pe.wait_ge(s_sadd, u)
                for place in range(GRP):
                    r = head_at(place)
                    part = slice(64 * (r % 2), 64 * (r % 2) + 64)
                    lo_c, lo_k = (0, (b - 1) * P) if b else (P, 0)
                    last = pe.matmul(bank(0, 2)[:, place * 256 + lo_c:place * 256 + 256],
                                     qT[part, b // 4, 2 * g + r // 2, b % 4 * P:(b % 4 + 1) * P], kT[part, g, lo_k:(b + 1) * P],
                                     start=True, stop=True)
                last.then_inc(s_sc, 1)

            def probs_transpose(u):
                pe.wait_ge(s_exp, u + 1)
                if u >= 1:
                    pe.wait_ge(s_pta, u)
                    pe.wait_ge(s_ptv, u)
                for place in range(GRP):
                    for kb in range(0 if u // NKV else 1, 2):
                        last = pe.transpose(bank(4, 2)[:, (place * 2 + kb) * P:(place * 2 + kb + 1) * P],
                                            scores[:, u % 2, place, kb * P:(kb + 1) * P], ident[:, :])
                last.then_inc(s_ptr, 1)

            def pv_product(u):
                b, g = u // NKV, u % NKV
                pe.wait_ge(s_pta, u + 1)
                pe.wait_ge(s_ptv, u + 1)
                if u >= 1:
                    pe.wait_ge(s_at, u)
                for place in range(GRP):
                    first = 0 if b else 1
                    for kb in range(first, 2):
                        last = pe.matmul(bank(6)[:, place * HD:(place + 1) * HD],
                                         probsT[:, u % 2, (place * 2 + kb) * P:(place * 2 + kb + 1) * P],
                                         vv[:, b - 1 + kb, g * HD:(g + 1) * HD], start=(kb == first), stop=(kb == 1))
                last.then_inc(s_pv, 1)

            def heads_transpose(u):
                pe.wait_ge(s_o, u + 1)
                for z in range(2):
                    last = pe.transpose(bank(6)[:, z * P:(z + 1) * P], heads[:, u % 2, z * P:(z + 1) * P], ident[:, :])
                last.then_inc(s_ot, 1)

            pe.wait_ge(s_qa, len(by_act))
            pe.wait_ge(s_qv, len(by_dve))
            pe.wait_ge(s_kd, NKV * 16)
            pe.wait_ge(s_gB, 1)
            scores_product(0)
            scores_product(1)

            def o_product(t, h):
                if t == 0:
                    pe.wait_ge(s_wo[h], 16)
                pe.wait_ge(s_at, 4 * t + 4)
                if t or h:
                    pe.wait_ge(s_x1, 2 * t + h)
                else:
                    pe.wait_ge(s_qa, len(by_act) + 2 * KT)
                for k in range(KT):
                    last = pe.matmul(bank(7), attnT[:, k, t * P:(t + 1) * P], wo[:, k, h * 512:h * 512 + 512],
                                     start=(k == 0), stop=(k == KT - 1))
                last.then_inc(s_op, 1)

            def q_product(m, z):
                pe.wait_ge(s_qa, len(by_act) + 2 * m + z)
                for k in range(KT):
                    last = pe.matmul(bank(7)[:, 0:256], wq[:, k, m * P:(m + 1) * P], hT[:, k, 512 + z * 256:768 + z * 256],
                                     start=(k == 0), stop=(k == KT - 1))
                last.then_inc(s_qkv, 1)

            def xn2_transpose(t, h):
                pe.wait_ge(s_xn2, t + 1)
                if t or h:
                    pe.wait_ge(s_h2a, 2 * t + h)
                for k in range(4):
                    last = pe.transpose(bank(2)[:, k * P:(k + 1) * P],
                                        xn2[:, t % 2, (4 * h + k) * P:(4 * h + k + 1) * P], ident[:, :])
                last.then_inc(s_x2, 1)

            def logits(t):
                pe.wait_ge(s_h2a, 2 * t + 2)
                if t >= 1:
                    pe.wait_ge(s_dest, t)
                for k in range(KT):
                    last = pe.matmul(bank(3)[:, 0:E], h2T[:, t % 2, k, :], wr[:, k, :], start=(k == 0), stop=(k == KT - 1))
                last.then_inc(s_lg, 1)

            def ranks(t):
                pe.wait_ge(s_mask, t + 1)
                last = pe.matmul(bank(3)[:, 0:E], tri[:, :], mask[:, t, :], start=True, stop=(t == 0))
                if t:
                    last = pe.matmul(bank(3)[:, 0:E], ones[:, :], macc[:, t - 1, :], start=False, stop=True)
                last.then_inc(s_rank, 1)

            for u in range(STEPS):
                if u < UNITS:
                    probs_transpose(u)
                if 1 <= u <= UNITS:
                    pv_product(u - 1)
                if u + 2 < UNITS:
                    scores_product(u + 2)
                if u in q_late:
                    q_product(*q_late[u])
                if u in o_half:
                    o_product(*o_half[u])
                if u in x2_half:
                    xn2_transpose(*x2_half[u])
                if u in logit_at:
                    logits(logit_at[u])
                if u in rank_at:
                    ranks(rank_at[u])
                if 1 <= u <= UNITS:
                    heads_transpose(u - 1)
            pe.wait_ge(s_dest, TT)
            pe.matmul(bank(3)[:, 64:64 + E], ones[:, :], macc[:, TT - 1, :], start=True, stop=True).then_inc(s_cnt, 1)
            pe.wait_ge(s_brow, 16)
            for r in range(6):
                last = pe.transpose(bank(0, 2)[:, r * P:(r + 1) * P], brow[:, r, :], ident[:, :])
            last.then_inc(s_bt, 1)

            def rows_transpose(n, kp):
                for k in range(2):
                    for b in range(2 if n > P else 1):
                        rows = min(n - b * P, P)
                        at = k * 256 + b * P
                        last = pe.transpose(bank(4 + kp % 2)[:, at:at + rows],
                                            xg[0:rows, b, (2 * kp + k) * P:(2 * kp + k + 1) * P], ident[0:rows, 0:rows])
                last.then_inc(s_xtp, 1)

            def last_tile_transpose(i):
                pe.wait_ge(s_me, i * 8 + 8)
                pe.wait_ge(s_ye, i * 5 + 3)
                pe.transpose(bank(7)[:, 0:P], yT[:, 7, P:2 * P], ident[:, :])
                pe.transpose(bank(7)[:, 3 * P:4 * P], yT[:, 7, 0:P], ident[:, :]).then_inc(s_ytp, 1)

            pe.wait_ge(s_bT, 1)
            pe.wait_ge(s_g, 32)
            rows_transpose(ITEM, 0)
            rows_transpose(ITEM, 1)
            pe.wait_ge(s_row, 16)
            n_items = pe.value_load(nrow, min_val=1, max_val=NITEM)

            def next_rows_transpose(i):
                pe.wait_ge(s_g, i * 32 + 64)
                rows_transpose(ITEM, 0)
                rows_transpose(ITEM, 1)

            def item(i, n, wide):
                pe.wait_ge(s_wl[0], i * 32 + 32)

                def up_product(j, s, k):
                    w = piece(j // 2).rearrange("p (k s n) -> p k s n", k=KT, s=2)
                    return pe.matmul(bank(j % 4)[:, s * 256:s * 256 + n], w[:, k, s, (j % 2) * P:(j % 2 + 1) * P],
                                     xT[:, k, 0:n], start=(k == 0), stop=(k == KT - 1))

                for k in range(KT):
                    pe.wait_ge(s_xT, i * 8 + k + 1)
                    for j in range(4):
                        if k == 0 and j == 2:
                            pe.wait_ge(s_wl[1], i * 32 + 32)
                        if k == 0 and j == 3:
                            pe.wait_ge(s_me, i * 8 + 8)
                        up_product(j, 0, k)
                    if k in (1, 2):
                        if k == 1:
                            pe.wait_ge(s_ye, i * 5 + 1)
                        else:
                            pe.wait_ge(s_xT, i * 8 + 4)
                        rows_transpose(n, k + 1)
                    if k == 2:
                        last_tile_transpose(i)
                for j in range(8):
                    if j >= 4:
                        if j % 2 == 0:
                            pe.wait_ge(s_wl[j // 2], i * 32 + 32)
                        pe.wait_ge(s_je, i * 8 + j - 3)
                        for k in range(KT):
                            up_product(j, 0, k)
                    for k in range(KT):
                        last = up_product(j, 1, k)
                    last.then_inc(s_mm, 1)
                for m in range(8):
                    if m % 4 == 0:
                        pe.wait_ge(s_wl[4 + m // 4], i * 16 + 16)
                    if m < 4:
                        pe.wait_ge(s_je, i * 8 + m + 5)
                    else:
                        pe.wait_ge(s_me, i * 8 + m + 5)
                    w = piece(4 + m // 4).rearrange("p (k n) -> p k n", k=KT)
                    for k in range(KT):
                        if m == 0:
                            pe.wait_ge(s_act, i * 8 + k + 1)
                        last = pe.matmul(bank(m % 4)[:, 0:n], w[:, k, (m % 4) * P:(m % 4 + 1) * P], actT[:, k, 0:n],
                                         start=(k == 0), stop=(k == KT - 1))
                    last.then_inc(s_mm, 1)
                    if wide and m == 4:
                        next_rows_transpose(i)
                pe.wait_ge(s_me, i * 8 + 15)
                if wide:
                    pe.sem_inc(s_pego, 1)
                for b, h, done in y_parts(wide):
                    rows = n - P if b else P
                    for m in range(4 * h, 4 + 3 * h):
                        last = pe.transpose(bank((4 if b else 6) + h)[0:rows, (m % 4) * P:(m % 4 + 1) * P],
                                            yT[:, m, b * P:b * P + rows], ident[:, :])
                    last.then_inc(s_ytp, done)
                if not wide:
                    next_rows_transpose(i)

            with pe.Fori(0, NITEM) as i:
                with pe.If(i < n_items):
                    width = pe.value_load(items[:, bass.ds(i * FIELDS + 2, 1)], min_val=0, max_val=len(WIDTHS) - 1)
                    by_width(pe, width, lambda w: item(i, WIDTHS[w], w >= NARROW))
                    with pe.If(i >= n_items - 1):
                        last_tile_transpose(i + 1)


def relative_constants():
    r = np.arange(RROW)
    dist = 2 * P - 1 - r
    n = np.maximum(dist, 0)
    exact = NBUCKET // 2
    large = exact + (np.log(np.maximum(n, 1) / exact) / np.log(P / exact) * (NBUCKET - exact) + 1e-9).astype(np.int64)
    bucket = np.where(n < exact, n, np.minimum(large, NBUCKET - 1))
    inside = (dist >= 0) & (dist < P)
    rows = ((bucket[None, :] == np.arange(NBUCKET)[:, None]) & inside[None, :]).astype(np.float32)
    fill = np.where(inside, np.float32(0), np.float32(NEG)).astype(np.float32)
    return rows, np.broadcast_to(fill, (NQ, RROW)).copy()


def kernel(x, c, w_mod, b_mod, norm_mix_g, norm_ffn_g, attn_w_qkv, attn_b_qkv, attn_w_o, attn_b_o,
           attn_sinks, rel_bias_table, conv_w_in, conv_b_in, conv_w_dw, conv_b_dw, conv_ln_g, conv_ln_b,
           conv_w_out, conv_b_out, router_w, router_b, moe_w_in, moe_b_in, moe_w_out, moe_b_out,
           final_norm_g):
    import concourse.bacc as _bacc
    from concourse.bass_utils import run_bass_kernel_spmd as _run

    def rows(*vectors):
        return np.concatenate([np.asarray(v).reshape(-1, P) for v in vectors], axis=0)

    bucket_rows, window_fill = relative_constants()
    ins = {
        "x": np.asarray(x)[0], "c": np.asarray(c), "w_mod": np.asarray(w_mod)[0],
        "vecs": rows(b_mod, norm_mix_g, norm_ffn_g, attn_b_qkv, attn_b_o),
        "w_qkv": np.asarray(attn_w_qkv)[0], "w_o": np.asarray(attn_w_o)[0],
        "sinks": np.asarray(attn_sinks)[0], "rel_table": np.asarray(rel_bias_table),
        "router_w": np.asarray(router_w)[0], "router_b": np.asarray(router_b)[0],
        "moe_w_in": np.asarray(moe_w_in)[0],
        "moe_b": np.concatenate([np.asarray(moe_b_in)[0].reshape(E, 16, P), np.asarray(moe_b_out)[0].reshape(E, 8, P)],
                                axis=1).reshape(E * 24, P),
        "moe_w_out": np.asarray(moe_w_out)[0], "final_g": np.asarray(final_norm_g),
        "bucket_rows": bucket_rows, "window_fill": window_fill,
    }
    nc = _bacc.Bacc("TRN2", target_bir_lowering=False, num_devices=1)
    arrays, args = {}, []
    for name, a in ins.items():
        a = np.ascontiguousarray(a)
        arrays[f"in_{name}"] = a
        args.append(nc.dram_tensor(f"in_{name}", a.shape, mybir.dt.from_np(a.dtype), kind="ExternalInput").ap())
    args.append(nc.dram_tensor("out_0", (SEQ, D), mybir.dt.float32, kind="ExternalOutput").ap())
    program(nc, *args)
    r = _run(nc, [arrays], core_ids=[0])
    return r.results[0]["out_0"].reshape(1, SEQ, D)
```
